# Optimizing a Trainium2 kernel written in Bass

```python
import jax, jax.numpy as jnp
from jax import lax
import numpy as np

D_MODEL = 1024
BATCH = 1
SEQ = 256
DEPTH = 2

D_RNN = 1408
RNN_BLOCKS = 16
RNN_BW = D_RNN // RNN_BLOCKS
CONV_WIDTH = 4
LRU_C = 8.0
N_HEADS = 16
HEAD_DIM = 64
N_KV_GROUPS = 4
HEADS_PER_GROUP = N_HEADS // N_KV_GROUPS
CMP_BLOCK = 32
CMP_STRIDE = 16
CMP_HIDDEN = 256
SEL_BLOCK = 64
N_SEL = 16
WINDOW = 512
Q_BLOCK = 128
SEL_Q_BLOCK = 32
FORCE_SCORE = 1.0e4
ROPE_THETA = 10000.0
NSA_IN = N_HEADS * HEAD_DIM + 6 * N_KV_GROUPS * HEAD_DIM + 3 * N_HEADS
D_FF = 3584
N_EXPERTS = 8
TOP_K = 2
RMS_EPS = 1e-6

kernel_name = "hybrid_rglru_nsa_moe_trunk"

def rmsnorm(x, g):
    xf = x.astype(jnp.float32)
    y = xf * lax.rsqrt(jnp.mean(xf * xf, axis=-1, keepdims=True) + RMS_EPS)
    return (y * g.astype(jnp.float32)).astype(x.dtype)

def rope(x, pos):
    half = HEAD_DIM // 2
    freqs = ROPE_THETA ** (-jnp.arange(half, dtype=jnp.float32) / half)
    ang = pos[:, None] * freqs[None, :]
    cos = jnp.cos(ang)[None, :, None, :].astype(x.dtype)
    sin = jnp.sin(ang)[None, :, None, :].astype(x.dtype)
    x1, x2 = x[..., :half], x[..., half:]
    return jnp.concatenate([x1 * cos - x2 * sin, x2 * cos + x1 * sin], axis=-1)

def masked_softmax(s, mask):
    s = jnp.where(mask, s.astype(jnp.float32), -jnp.inf)
    m = jnp.max(s, axis=-1, keepdims=True)
    m = jnp.where(jnp.isfinite(m), m, 0.0)
    e = jnp.where(mask, jnp.exp(s - m), 0.0)
    return e / jnp.maximum(jnp.sum(e, axis=-1, keepdims=True), 1e-30)

def rglru_mixer(x, w_in, b_in, conv_w, conv_b, w_a, b_a, w_i, b_i, lam, w_out, b_out):
    B, S, _ = x.shape
    proj = x @ w_in + b_in
    gate, xr = jnp.split(proj, 2, axis=-1)
    gate = jax.nn.gelu(gate)
    xp = jnp.pad(xr, ((0, 0), (CONV_WIDTH - 1, 0), (0, 0)))
    xc = conv_b + sum(xp[:, k:k + S] * conv_w[k] for k in range(CONV_WIDTH))
    xb = xc.reshape(B, S, RNN_BLOCKS, RNN_BW)
    r = jax.nn.sigmoid(jnp.einsum('bsnc,ncd->bsnd', xb, w_a).reshape(B, S, D_RNN) + b_a)
    i = jax.nn.sigmoid(jnp.einsum('bsnc,ncd->bsnd', xb, w_i).reshape(B, S, D_RNN) + b_i)
    log_a = (-LRU_C * r.astype(jnp.float32)) * jax.nn.softplus(-lam.astype(jnp.float32))
    a = jnp.exp(log_a)
    mult = jnp.sqrt(-jnp.expm1(2.0 * log_a))
    mult = mult.at[:, 0].set(1.0)
    u = mult * (i * xc).astype(jnp.float32)

    def combine(lhs, rhs):
        a1, b1 = lhs
        a2, b2 = rhs
        return a1 * a2, a2 * b1 + b2

    _, h = lax.associative_scan(combine, (a, u), axis=1)
    y = h.astype(x.dtype) * gate
    return y @ w_out + b_out

def compress(t, pe, w1, w2):
    B, S, G, D = t.shape
    r = CMP_BLOCK // CMP_STRIDE
    n_ch = S // CMP_STRIDE
    ch = t.reshape(B, n_ch, CMP_STRIDE, G, D)
    blk = jnp.concatenate([ch[:, j:n_ch - r + 1 + j] for j in range(r)], axis=2)
    blk = blk + pe[None, None, :, None, :]
    flat = blk.transpose(0, 1, 3, 2, 4).reshape(B, n_ch - r + 1, G, CMP_BLOCK * D)
    return jax.nn.gelu(flat @ w1) @ w2

def overlap_matrix(n_c, n_s):
    r = CMP_BLOCK // CMP_STRIDE
    qn = SEL_BLOCK // CMP_STRIDE
    chunks = np.arange(n_c)[:, None] + np.arange(r)[None, :]
    m = np.zeros((n_c, n_s), np.float32)
    np.add.at(m, (np.repeat(np.arange(n_c), r), (chunks // qn).ravel()), 1.0)
    return m

def nsa_mixer(x, w_in, cmp_pe, cmp_w1, cmp_w2, w_out):
    B, S, _ = x.shape
    H, G, HP, DH = N_HEADS, N_KV_GROUPS, HEADS_PER_GROUP, HEAD_DIM
    proj = x @ w_in
    cuts = list(np.cumsum([H * DH] + [G * DH] * 6))
    q, kc, vc, ks, vs, kw, vw, g = jnp.split(proj, cuts, axis=-1)
    q = q.reshape(B, S, H, DH)
    kc, vc, ks, vs, kw, vw = [t.reshape(B, S, G, DH) for t in (kc, vc, ks, vs, kw, vw)]
    gates = jax.nn.sigmoid(g.reshape(B, S, H, 3))
    pos = jnp.arange(S, dtype=jnp.float32)
    q = rope(q, pos) * (DH ** -0.5)
    kc, ks, kw = rope(kc, pos), rope(ks, pos), rope(kw, pos)
    qg = q.reshape(B, S, G, HP, DH)

    k_cmp = compress(kc, cmp_pe[0], cmp_w1[0], cmp_w2[0])
    v_cmp = compress(vc, cmp_pe[1], cmp_w1[1], cmp_w2[1])
    n_c = k_cmp.shape[1]
    n_s = S // SEL_BLOCK
    k_sel = min(N_SEL, n_s)
    cmp_end = jnp.arange(n_c) * CMP_STRIDE + CMP_BLOCK - 1
    blk_start = jnp.arange(n_s) * SEL_BLOCK
    overlap = jnp.asarray(overlap_matrix(n_c, n_s))

    def cmp_block(i):
        s0 = i * Q_BLOCK
        qb = lax.dynamic_slice_in_dim(qg, s0, Q_BLOCK, axis=1)
        t = s0 + jnp.arange(Q_BLOCK)
        sc = jnp.einsum('bqghd,bcgd->bghqc', qb, k_cmp)
        p = masked_softmax(sc, cmp_end[None, :] <= t[:, None])
        o = jnp.einsum('bghqc,bcgd->bqghd', p.astype(v_cmp.dtype), v_cmp)
        imp = jnp.einsum('bghqc,cn->bgqn', p, overlap)
        cur = t[:, None] // SEL_BLOCK
        j = jnp.arange(n_s)[None, :]
        forced = (j == 0) | (j == cur) | (j == cur - 1)
        valid = blk_start[None, :] <= t[:, None]
        score = jnp.where(forced, FORCE_SCORE, jnp.where(valid, imp, -1.0))
        _, idx = lax.top_k(score, k_sel)
        return o, idx

    o_cmp, sel_idx = lax.map(cmp_block, jnp.arange(S // Q_BLOCK))
    o_cmp = o_cmp.transpose(1, 0, 2, 3, 4, 5).reshape(B, S, H, DH)
    sel_idx = sel_idx.transpose(1, 2, 0, 3, 4).reshape(B, G, S, k_sel)

    kb = ks.reshape(B, n_s, SEL_BLOCK, G, DH).transpose(0, 3, 1, 2, 4)
    vb = vs.reshape(B, n_s, SEL_BLOCK, G, DH).transpose(0, 3, 1, 2, 4)
    bi = jnp.arange(B)[:, None, None, None]
    gi = jnp.arange(G)[None, :, None, None]

    def sel_block(i):
        s0 = i * SEL_Q_BLOCK
        qb = lax.dynamic_slice_in_dim(qg, s0, SEL_Q_BLOCK, axis=1)
        idx = lax.dynamic_slice_in_dim(sel_idx, s0, SEL_Q_BLOCK, axis=2)
        t = s0 + jnp.arange(SEL_Q_BLOCK)
        kg = kb[bi, gi, idx]
        vg = vb[bi, gi, idx]
        sc = jnp.einsum('bqghd,bgqkld->bghqkl', qb, kg)
        kpos = idx[..., None] * SEL_BLOCK + jnp.arange(SEL_BLOCK)
        mask = kpos <= t[None, None, :, None, None]
        n_k = k_sel * SEL_BLOCK
        p = masked_softmax(sc.reshape(B, G, HP, SEL_Q_BLOCK, n_k),
                           mask[:, :, None].reshape(B, G, 1, SEL_Q_BLOCK, n_k))
        return jnp.einsum('bghqn,bgqnd->bqghd', p.astype(vg.dtype),
                          vg.reshape(B, G, SEL_Q_BLOCK, n_k, DH))

    o_sel = lax.map(sel_block, jnp.arange(S // SEL_Q_BLOCK))
    o_sel = o_sel.transpose(1, 0, 2, 3, 4, 5).reshape(B, S, H, DH)

    kw_p = jnp.pad(kw, ((0, 0), (WINDOW, 0), (0, 0), (0, 0)))
    vw_p = jnp.pad(vw, ((0, 0), (WINDOW, 0), (0, 0), (0, 0)))
    span = WINDOW + Q_BLOCK

    def win_block(i):
        s0 = i * Q_BLOCK
        qb = lax.dynamic_slice_in_dim(qg, s0, Q_BLOCK, axis=1)
        kb_ = lax.dynamic_slice_in_dim(kw_p, s0, span, axis=1)
        vb_ = lax.dynamic_slice_in_dim(vw_p, s0, span, axis=1)
        t = s0 + jnp.arange(Q_BLOCK)
        kpos = s0 - WINDOW + jnp.arange(span)
        d = t[:, None] - kpos[None, :]
        mask = (kpos[None, :] >= 0) & (d >= 0) & (d < WINDOW)
        sc = jnp.einsum('bqghd,bkgd->bghqk', qb, kb_)
        p = masked_softmax(sc, mask)
        return jnp.einsum('bghqk,bkgd->bqghd', p.astype(vb_.dtype), vb_)

    o_win = lax.map(win_block, jnp.arange(S // Q_BLOCK))
    o_win = o_win.transpose(1, 0, 2, 3, 4, 5).reshape(B, S, H, DH)

    gates = gates.astype(x.dtype)
    o = gates[..., 0, None] * o_cmp + gates[..., 1, None] * o_sel + gates[..., 2, None] * o_win
    return o.reshape(B, S, H * DH) @ w_out

def swiglu(x, w_gate, w_up, w_down):
    return (jax.nn.silu(x @ w_gate) * (x @ w_up)) @ w_down

def moe_ffn(x, w_router, w_gate, w_up, w_down):
    B, S, D = x.shape
    xt = x.reshape(B * S, D)
    logits = (xt @ w_router).astype(jnp.float32)
    top_v, top_i = lax.top_k(logits, TOP_K)
    top_w = jax.nn.softmax(top_v, axis=-1)
    gates = jnp.sum(jax.nn.one_hot(top_i, N_EXPERTS, dtype=jnp.float32) * top_w[..., None], axis=1)
    gates = gates.astype(x.dtype)
    out = jnp.zeros_like(xt)
    for e in range(N_EXPERTS):
        out = out + gates[:, e:e + 1] * swiglu(xt, w_gate[e], w_up[e], w_down[e])
    return out.reshape(B, S, D)

def setup_inputs(seed: int = 0) -> dict:
    key = jax.random.key(seed)
    ks = iter(jax.random.split(key, 40))
    n_a = (DEPTH + 1) // 2
    n_b = DEPTH // 2
    f32 = jnp.float32

    def nrm(shape, fan_in):
        return jax.random.normal(next(ks), shape, f32) * (fan_in ** -0.5)

    def small(shape, s=0.02):
        return jax.random.normal(next(ks), shape, f32) * s

    u = jax.random.uniform(next(ks), (n_a, D_RNN), f32, minval=0.9, maxval=0.999)
    s = u ** (1.0 / LRU_C)
    lam = jnp.log(s) - jnp.log1p(-s)
    return {
        "x": jax.random.normal(next(ks), (BATCH, SEQ, D_MODEL), f32),
        "norm_mix": 1.0 + small((DEPTH, D_MODEL), 0.05),
        "norm_ffn": 1.0 + small((DEPTH, D_MODEL), 0.05),
        "norm_final": 1.0 + small((D_MODEL,), 0.05),
        "lru_w_in": nrm((n_a, D_MODEL, 2 * D_RNN), D_MODEL),
        "lru_b_in": small((n_a, 2 * D_RNN)),
        "lru_conv_w": nrm((n_a, CONV_WIDTH, D_RNN), CONV_WIDTH),
        "lru_conv_b": small((n_a, D_RNN)),
        "lru_w_a": nrm((n_a, RNN_BLOCKS, RNN_BW, RNN_BW), RNN_BW),
        "lru_b_a": small((n_a, D_RNN), 0.1),
        "lru_w_i": nrm((n_a, RNN_BLOCKS, RNN_BW, RNN_BW), RNN_BW),
        "lru_b_i": small((n_a, D_RNN), 0.1),
        "lru_lambda": lam,
        "lru_w_out": nrm((n_a, D_RNN, D_MODEL), D_RNN),
        "lru_b_out": small((n_a, D_MODEL)),
        "nsa_w_in": nrm((n_b, D_MODEL, NSA_IN), D_MODEL),
        "nsa_cmp_pe": small((n_b, 2, CMP_BLOCK, HEAD_DIM), 0.1),
        "nsa_cmp_w1": nrm((n_b, 2, CMP_BLOCK * HEAD_DIM, CMP_HIDDEN), CMP_BLOCK * HEAD_DIM),
        "nsa_cmp_w2": nrm((n_b, 2, CMP_HIDDEN, HEAD_DIM), CMP_HIDDEN),
        "nsa_w_out": nrm((n_b, N_HEADS * HEAD_DIM, D_MODEL), N_HEADS * HEAD_DIM),
        "ffn_w_gate": nrm((n_a, D_MODEL, D_FF), D_MODEL),
        "ffn_w_up": nrm((n_a, D_MODEL, D_FF), D_MODEL),
        "ffn_w_down": nrm((n_a, D_FF, D_MODEL), D_FF),
        "moe_w_router": nrm((n_b, D_MODEL, N_EXPERTS), D_MODEL),
        "moe_w_gate": nrm((n_b, N_EXPERTS, D_MODEL, D_FF), D_MODEL),
        "moe_w_up": nrm((n_b, N_EXPERTS, D_MODEL, D_FF), D_MODEL),
        "moe_w_down": nrm((n_b, N_EXPERTS, D_FF, D_MODEL), D_FF),
    }

def reference(x, norm_mix, norm_ffn, norm_final,
              lru_w_in, lru_b_in, lru_conv_w, lru_conv_b, lru_w_a, lru_b_a,
              lru_w_i, lru_b_i, lru_lambda, lru_w_out, lru_b_out,
              nsa_w_in, nsa_cmp_pe, nsa_cmp_w1, nsa_cmp_w2, nsa_w_out,
              ffn_w_gate, ffn_w_up, ffn_w_down,
              moe_w_router, moe_w_gate, moe_w_up, moe_w_down):
    for layer in range(DEPTH):
        j = layer // 2
        h = rmsnorm(x, norm_mix[layer])
        if layer % 2 == 0:
            x = x + rglru_mixer(h, lru_w_in[j], lru_b_in[j], lru_conv_w[j], lru_conv_b[j],
                                lru_w_a[j], lru_b_a[j], lru_w_i[j], lru_b_i[j],
                                lru_lambda[j], lru_w_out[j], lru_b_out[j])
            h = rmsnorm(x, norm_ffn[layer])
            x = x + swiglu(h, ffn_w_gate[j], ffn_w_up[j], ffn_w_down[j])
        else:
            x = x + nsa_mixer(h, nsa_w_in[j], nsa_cmp_pe[j], nsa_cmp_w1[j], nsa_cmp_w2[j],
                              nsa_w_out[j])
            h = rmsnorm(x, norm_ffn[layer])
            x = x + moe_ffn(h, moe_w_router[j], moe_w_gate[j], moe_w_up[j], moe_w_down[j])
    return rmsnorm(x, norm_final)


_drawn_inputs = setup_inputs


def setup_inputs(seed=0):
    import zlib

    import numpy as np

    out = dict(_drawn_inputs(seed))
    spreads = {}
    factors = {}
    for name, (base, spread) in spreads.items():
        noise = np.random.default_rng([zlib.crc32(name.encode()), seed]).standard_normal(out[name].shape)
        drawn = base * np.exp(spread * noise) if base else spread * noise
        out[name] = __import__('jax').numpy.asarray(drawn.astype(out[name].dtype))
    for name, factor in factors.items():
        out[name] = (out[name] * factor).astype(out[name].dtype)
    return out
```

```python
from contextlib import ExitStack

import concourse.bass as bass
from concourse import mybir

F32 = mybir.dt.float32
BF16 = mybir.dt.bfloat16
U32 = mybir.dt.uint32
I32 = mybir.dt.int32
ALU = mybir.AluOpType
ACT = mybir.ActivationFunctionType
AX = mybir.AxisListType.X

P = 128
D = 1024
KD = D // P
S = 256
TB = S // P
RNN = 1408
RT = RNN // P
LRU_C = 8.0
BW = 88
CONV = 4
FF = 3584
NCH = FF // P
E = 8
CAP = 96
MAXOV = 5
H, G, HP, DH = 16, 4, 4, 64
NC = 15
CB, CS = 32, 16
HID = 256
QKV = 3 * 2 * G * DH + H * DH + 3 * H
NIN = 7
CG = 384
EPS = 1e-6
MAXP = E + MAXOV
NEG = -1e30

NS = 14
SW = 3072
HALF = NCH // NS

PAIRS = [(i, j) for j in range(RT) for i in range(RT)
         if any(b * BW < (i + 1) * P and (b + 1) * BW > i * P and b * BW < (j + 1) * P and (b + 1) * BW > j * P
                for b in range(RNN // BW))]
BD_TILES = 2 * len(PAIRS)
BD_ITEMS = -(-BD_TILES * P // SW)

C_ID, C_TRI, C_ONE, C_CAU = 0, 128, 256, 384
C_COS, C_SIN, C_COSQ, C_SINQ = 512, 640, 768, 896
C_CM, C_CV = 1024, 1024 + TB * NC
C_IOTA = C_CV + TB * NC
NCONST = C_IOTA + CAP
W_BX, W_BG, W_CW, W_CB, W_BA, W_BI, W_LAM = 0, RT, 2 * RT, 6 * RT, 7 * RT, 8 * RT, 9 * RT
W_PE = 10 * RT
W_RT = W_PE + 32
NPAR = W_RT + KD * E



LRU_ORDER = [("lru", 0), ("lru", 1), ("lru", 2), ("lru", 3)] + [("bd", i) for i in range(BD_ITEMS)] + \
            [("lru", 4), ("lru", 5), ("lru", 6), ("lru", 7)] + [("lout", i) for i in range(4)]
NSA_ORDER = [("qkv", i) for i in range(NIN)] + [("cmp", i) for i in range(3)] + [("nout", i) for i in range(3)]
LRU_SLOTS = 10
FFN0 = 5
NSA_SLOTS = [5, 6, 7, 8, 9, 10, 11, 5, 6, 7, 9, 10, 11]


def plan_ring():
    items, last = [], {}

    def add(kind, i, s):
        items.append((kind, i, s, last.get(s)))
        last[s] = len(items) - 1

    for n, (kind, i) in enumerate(LRU_ORDER):
        add(kind, i, n % LRU_SLOTS)
    for s in range(LRU_SLOTS, NS):
        last[s] = len(items) - 1
    for c in range(NCH):
        add("ffn", c, (FFN0 + c) % NS)
    for (kind, i), s in zip(NSA_ORDER, NSA_SLOTS):
        add(kind, i, s)
    for s in (12, 13, 0, 1, 2, 3, 4):
        last[s] = len(items) - 1
    return items, [last[(FFN0 + c) % NS] for c in range(NS)]


ITEMS, MOE_AFTER = plan_ring()
INDEX = {(kind, i): n for n, (kind, i, s, a) in enumerate(ITEMS)}
SLOT = {(kind, i): s for kind, i, s, a in ITEMS}
LOADS = [sum(1 for it in ITEMS if it[2] == s) for s in range(NS)]
MOE_AT = len(ITEMS)


def nth_load(kind, i):
    n = INDEX[(kind, i)]
    return sum(1 for it in ITEMS[:n + 1] if it[2] == SLOT[(kind, i)])


def build(nc, x, consts, params, rows, w_lru, w_bd, w_lout, w_ffn, w_qkv, w_cmp, w_nout, w_moe, out):
    with ExitStack() as ctx:
        def sb(name, shape, dt=F32):
            return ctx.enter_context(nc.sbuf_tensor(name, shape, dt))

        ring = sb("ring", [P, NS * SW])
        xs = sb("xs", [P, TB, D])
        hn = sb("hn", [P, TB, D])
        hT = sb("hT", [P, KD, S])
        con = sb("con", [P, NCONST])
        par = sb("par", [P, NPAR])
        row = sb("row", [P, 2, D])
        arena = sb("arena", [P, 1536])
        stat = sb("stat", [P, 16])
        zer = sb("zer", [P, 512], BF16)
        act_g = sb("act_g", [P, 2, S])
        hid = sb("hid", [P, 2, S])
        rt = sb("rt", [P, 360])
        ovt = sb("ovt", [P, 8], I32)
        topi = sb("topi", [P, TB, 8], U32)
        ps = ctx.enter_context(nc.psum_tensor("ps", [P, 8, 512], F32))

        ident = con[:, C_ID:C_ID + P]
        tri = con[:, C_TRI:C_TRI + P]
        ones = con[:, C_ONE:C_ONE + P]
        causal = con[:, C_CAU:C_CAU + P]

        def ring_slot(s):
            return ring[:, s * SW:(s + 1) * SW]

        def item(kind, i):
            return ring_slot(SLOT[(kind, i)])

        gate_t = ring_slot(10)[:, 0:RT * S].rearrange("p (j t) -> p j t", j=RT)
        xc_t = ring_slot(11)[:, 0:RT * S].rearrange("p (j t) -> p j t", j=RT)
        th_t = ring_slot(12)[:, 0:RT * S].rearrange("p (j t) -> p j t", j=RT)
        u_t = ring_slot(13)[:, 0:RT * S].rearrange("p (j t) -> p j t", j=RT)
        xr_t = [arena[:, 260 * i:260 * i + CONV - 1 + S] for i in range(2)]
        r_t = [arena[:, 520 + S * i:520 + S * (i + 1)] for i in range(2)]
        lam_t = [arena[:, 1040 + 16 * i:1040 + 16 * i + RT] for i in range(6)]

        k_t = ring_slot(12)[:, 0:TB * 768].rearrange("p (b c) -> p b c", b=TB)
        gates = ring_slot(12)[:, 1536:1632].rearrange("p (b r h) -> p b r h", b=TB, r=3)
        vc_t = ring_slot(12)[:, 1664:2176].rearrange("p (b c) -> p b c", b=TB)
        pc_t = ring_slot(12)[:, 2176:2688].rearrange("p (h c) -> p h c", h=H)
        q_t = hn
        rope_a, rope_b = [[arena[:, 768 * i + c:768 * i + c + CG].rearrange("p (h d) -> p h d", d=DH)
                           for i in range(2)] for c in (0, CG)]
        mx = [arena[:, 768 + 8 * i:772 + 8 * i] for i in range(2)]
        rc = arena[:, 784:788]
        cmx = arena[:, 800:816]
        csum = arena[:, 816:832]
        o_rw = arena[:, 896:1152].rearrange("p (f r d) -> p f r d", f=2, r=2)
        o_w = arena[:, 1152:1280].rearrange("p (f d) -> p f d", f=2)
        v65 = ring_slot(13)[:, 0:TB * 8 * 65].rearrange("p (b h d) -> p b h d", b=TB, d=65)
        vbd = ring_slot(13)[:, 1040:1552].rearrange("p (a j d) -> p a j d", a=2, j=4)
        hid_k = ring_slot(13)[:, 1552:1672]
        hid_v = ring_slot(13)[:, 1680:2704].rearrange("p (m g j c) -> p m g j c", m=2, g=G, j=4)
        kcT = ring_slot(13)[:, 2704:2764]
        qT = ring_slot(0)[:, 0:KD * S].rearrange("p (n t) -> p n t", n=KD)
        kT = ring_slot(1)[:, 0:1024].rearrange("p (r a t) -> p r a t", r=2, a=2)
        pcT = ring_slot(1)[:, 1024:1536].rearrange("p (g t) -> p g t", g=4)
        o_c = ring_slot(1)[:, 1536:1536 + D]
        kv2T = ring_slot(2)[:, 0:2048].rearrange("p (w g t) -> p w g t", w=2, g=G)
        o_t = ring_slot(2)[:, 0:2048].rearrange("p (b c) -> p b c", b=TB)
        flat = ring_slot(3)[:, 0:1920].rearrange("p (w i g c) -> p w i g c", w=2, i=16, g=G)
        oT = ring_slot(3)[:, 0:2048].rearrange("p (n t) -> p n t", n=KD)
        twice = ring_slot(4)[:, 0:2048].rearrange("p (w b g i d) -> p w b g i d", w=2, b=TB, g=G, i=2)
        p_t = ring_slot(4)[:, 0:2048].rearrange("p (u f r k) -> p u f r k", u=2, f=2, r=2)
        pT = hT[:, :, :].rearrange("p n t -> p (n t)").rearrange("p (u f r t) -> p u f r t", u=2, f=2, r=2)

        hT_flat = hT[:, :, :].rearrange("p n t -> p (n t)")
        sel = hT_flat[:, 0:TB * CAP].rearrange("p (b s) -> p b s", b=TB)
        selw = hT_flat[:, 192:192 + TB * CAP].rearrange("p (b s) -> p b s", b=TB)
        selwT = hT_flat[:, 384:640]
        xeT = hT_flat[:, 640:640 + KD * CAP].rearrange("p (n t) -> p n t", n=KD)
        yT = arena[:, 0:KD * CAP].rearrange("p (n t) -> p n t", n=KD)
        y_t = row[:, 0, :]
        lg = rt[:, 0:16].rearrange("p (b e) -> p b e", b=TB)
        m8 = rt[:, 16:32].rearrange("p (b e) -> p b e", b=TB)
        idx = rt[:, 32:48].rearrange("p (b e) -> p b e", b=TB)
        dv, ev, den, w1, w2 = [rt[:, 48 + 2 * i:50 + 2 * i] for i in range(5)]
        oh1, oh2, asg = [rt[:, 64 + 16 * i:80 + 16 * i].rearrange("p (b e) -> p b e", b=TB) for i in range(3)]
        posp = rt[:, 112:140].rearrange("p (b e) -> p b e", b=TB)
        wp = rt[:, 140:168].rearrange("p (b e) -> p b e", b=TB)
        ov, ov2, cum, cex = [rt[:, 168 + 8 * i:176 + 8 * i] for i in range(4)]
        cmp_t = rt[:, 200:240].rearrange("p (k e) -> p k e", e=E)
        ek, cxk, off = [rt[:, 240 + 8 * i:240 + 8 * i + MAXOV] for i in range(3)]
        ohk = rt[:, 264:304].rearrange("p (k e) -> p k e", e=E)
        prod = rt[:, 304:344].rearrange("p (k e) -> p k e", e=E)
        iota8 = con[:, C_IOTA:C_IOTA + E]
        iota5 = con[:, C_IOTA:C_IOTA + MAXOV]
        iota = con[:, C_IOTA:C_IOTA + CAP]

        def sem(name):
            return ctx.enter_context(nc.semaphore(name))

        class on:
            x_in = sem("x_in")
            const_in = sem("const_in")
            out_done = sem("out_done")
            used = sem("used")
            zero_set = sem("zero_set")
            norm_sq = sem("norm_sq")
            norm_ms = sem("norm_ms")
            norm_rms = sem("norm_rms")
            norm_hn = sem("norm_hn")
            norm_tr = sem("norm_tr")
            norm_hTa = sem("norm_hTa")
            norm_hTv = sem("norm_hTv")
            lam_abs = sem("lam_abs")
            lam_exp = sem("lam_exp")
            lam_sp = sem("lam_sp")
            xr_ps = sem("xr_ps")
            xr_sb = sem("xr_sb")
            conv_done = sem("conv_done")
            bd_ps = sem("bd_ps")
            r_done = sem("r_done")
            ig_done = sem("ig_done")
            th_done = sem("th_done")
            u_done = sem("u_done")
            sqrt_done = sem("sqrt_done")
            sqrt_used = sem("sqrt_used")
            gate_ps = sem("gate_ps")
            gate_done = sem("gate_done")
            y_done = sem("y_done")
            bias_done = sem("bias_done")
            x_done = sem("x_done")
            gu_ready = sem("gu_ready")
            silu_done = sem("silu_done")
            hid_ready = sem("hid_ready")
            qkv_ps = sem("qkv_ps")
            rope_done = sem("rope_done")
            v_done = sem("v_done")
            gates_done = sem("gates_done")
            twice_done = sem("twice_done")
            hid_v_done = sem("hid_v_done")
            cT_ps = sem("cT_ps")
            cT_done = sem("cT_done")
            flat_done = sem("flat_done")
            ch_ps = sem("ch_ps")
            ch_done = sem("ch_done")
            kc_ps = sem("kc_ps")
            vc_ps = sem("vc_ps")
            kc_done = sem("kc_done")
            vc_done = sem("vc_done")
            kT_ps = sem("kT_ps")
            kT_done = sem("kT_done")
            qT_ps = sem("qT_ps")
            qT_done = sem("qT_done")
            sc_ps = sem("sc_ps")
            sc_sub = sem("sc_sub")
            pc_exp = sem("pc_exp")
            pc_done = sem("pc_done")
            pcT_ps = sem("pcT_ps")
            pcT_done = sem("pcT_done")
            oc_ps = sem("oc_ps")
            oc_done = sem("oc_done")
            s_ps = sem("s_ps")
            s_max = sem("s_max")
            p_done = sem("p_done")
            pTa_ps = sem("pTa_ps")
            pTv_ps = sem("pTv_ps")
            pTa_done = sem("pTa_done")
            pTv_done = sem("pTv_done")
            o_ps = sem("o_ps")
            o_done = sem("o_done")
            oT_ps = sem("oT_ps")
            oTa_done = sem("oTa_done")
            oTv_done = sem("oTv_done")
            logit_ps = sem("logit_ps")
            top_diff = sem("top_diff")
            top_exp = sem("top_exp")
            asg_done = sem("asg_done")
            pos_ps = sem("pos_ps")
            ov_ready = sem("ov_ready")
            sel_ready = sem("sel_ready")
            selw_ready = sem("selw_ready")
            gathered = sem("gathered")
            xe_ready = sem("xe_ready")
            yT_ready = sem("yT_ready")
            wT_ps = sem("wT_ps")
            wT_ready = sem("wT_ready")
            y_ps = sem("y_ps")
            y_ready = sem("y_ready")
            comb_ps = sem("comb_ps")
            comb_done = sem("comb_done")
            dve_step = sem("dve_step")

        landed = [ctx.enter_context(nc.semaphore(f"landed{s}")) for s in range(NS)]
        row_in = [ctx.enter_context(nc.semaphore(f"row_in{i}")) for i in range(2)]
        block = ctx.enter_context(nc.Block())

        def weights(eng, kind, i):
            eng.wait_ge(landed[SLOT[(kind, i)]], 16 * nth_load(kind, i))

        @block.sync
        def _(sp):
            xv = x.rearrange("a (b p) d -> p (a b) d", p=P)
            sp.dma_start(xs[:, :, :], xv).then_inc(on.x_in, 16)
            sp.dma_start(con[:, :], consts).then_inc(on.const_in, 16)
            sp.dma_start(par[:, :], params).then_inc(on.const_in, 16)
            sp.dma_start(row[:, 0, :], rows[0:1, :].to_broadcast([P, D])).then_inc(row_in[0], 16)
            sources = {"lru": w_lru, "bd": w_bd, "lout": w_lout, "ffn": w_ffn, "qkv": w_qkv, "cmp": w_cmp,
                       "nout": w_nout}
            for n, (kind, i, s, after) in enumerate(ITEMS):
                if after is not None:
                    sp.wait_ge(on.used, after + 1)
                sp.dma_start(ring_slot(s), sources[kind][i]).then_inc(landed[s], 16)
                if n == 3:
                    sp.dma_start(row[:, 1, :], rows[1:2, :].to_broadcast([P, D])).then_inc(row_in[1], 16)
            for c in range(NS):
                s = (FFN0 + c) % NS
                sp.wait_ge(on.used, MOE_AFTER[c] + 1)
                sp.dma_start(ring_slot(s), w_moe[c]).then_inc(landed[s], 16)
            with sp.Fori(1, E * HALF) as turn:
                for c in range(NS):
                    s = (FFN0 + c) % NS
                    sp.wait_ge(on.used, turn * NS + (MOE_AT + c - NS + 1))
                    sp.dma_start(ring_slot(s), w_moe[bass.ds(turn * NS + c, 1)].rearrange("a p n -> p (a n)")
                                 ).then_inc(landed[s], 16)
            sp.wait_ge(on.ov_ready, 1)
            further = sp.value_load(ovt[0:1, 0:1], min_val=0, max_val=MAXOV)
            with sp.If(further > 0):
                with sp.Fori(0, further) as k:
                    e = sp.value_load(ovt[0:1, bass.ds(k + 1, 1)], min_val=0, max_val=E - 1)
                    for i in range(HALF):
                        for c in range(NS):
                            s = (FFN0 + c) % NS
                            sp.wait_ge(on.used, k * NCH + (MOE_AT + E * NCH + i * NS + c - NS + 1))
                            sp.dma_start(ring_slot(s), w_moe[bass.ds(e * NCH + (i * NS + c), 1)]
                                         .rearrange("a p n -> p (a n)")).then_inc(landed[s], 16)

        @block.tensor
        def _(pe):
            def mm(o, a, b, start=True, stop=True):
                return nc.tensor.matmul(o, a, b, start=start, stop=stop, skip_group_check=True)

            def flip(o, a):
                return nc.tensor.transpose(o, a, ident)

            def norm_transposes(n):
                for b in range(TB):
                    pe.wait_ge(on.norm_hn, TB * n + b + 1)
                    for q in range(2):
                        for k in range(4):
                            last = flip(ps[:, 4 + 2 * b + q, k * P:(k + 1) * P],
                                        hn[:, b, (4 * q + k) * P:(4 * q + k + 1) * P])
                        last.then_inc(on.norm_tr, 1)
                pe.wait_ge(on.norm_hTa, TB * (n + 1))
                pe.wait_ge(on.norm_hTv, TB * (n + 1))

            def open_banks(banks, n):
                for k in banks:
                    mm(ps[:, k, 0:n], zer[:, 0:P], zer[:, 0:n])

            pe.wait_ge(on.const_in, 32)
            norm_transposes(0)

            def lru_tile(t, bank, used_up):
                weights(pe, "lru", t // 3)
                w = item("lru", t // 3)[:, t % 3 * D:(t % 3 + 1) * D].rearrange("p (k c) -> p k c", k=KD)
                for k in range(KD):
                    last = mm(ps[:, bank, 0:S], w[:, k, :], hT[:, k, :], k == 0, k == KD - 1)
                    if k == 0 and used_up:
                        last.then_inc(on.used, used_up)
                return last

            for j in range(RT):
                if j >= 4:
                    pe.wait_ge(on.xr_sb, j - 3)
                lru_tile(j, j % 4, 1 if j and j % 3 == 0 else 0).then_inc(on.xr_ps, 1)
            t = 0
            for j in range(RT):
                near = [i for i, jj in PAIRS if jj == j]
                pe.wait_ge(on.conv_done, max(near) + 1)
                if j >= 4:
                    pe.wait_ge(on.ig_done, j - 3)
                for w in range(2):
                    for i in near:
                        if t % (SW // P) == 0:
                            weights(pe, "bd", t // (SW // P))
                        o = t % (SW // P) * P
                        last = mm(ps[:, 4 + j % 4, w * S:(w + 1) * S],
                                  item("bd", t // (SW // P))[:, o:o + P], xc_t[:, i, :],
                                  i == near[0], i == near[-1])
                        t += 1
                last.then_inc(on.bd_ps, 1)
            for j in range(RT):
                if j >= 4:
                    pe.wait_ge(on.gate_done, j - 3)
                used_up = 1 + BD_ITEMS if j == 1 else 1 if (RT + j) % 3 == 0 and j > 1 else 0
                lru_tile(RT + j, j % 4, used_up).then_inc(on.gate_ps, 1)
            for k in range(RT):
                pe.wait_ge(on.y_done, k + 1)
                weights(pe, "lout", k // 3)
                w = item("lout", k // 3)[:, k % 3 * D:(k % 3 + 1) * D]
                for b in range(TB):
                    for h in range(2):
                        last = mm(ps[:, 4 + 2 * b + h, :], xc_t[:, k, b * P:(b + 1) * P],
                                  w[:, h * 512:(h + 1) * 512], k == 0, k == RT - 1)
                        if k == b == h == 0:
                            last.then_inc(on.used, 1)
                if k % 3 == 2 or k == RT - 1:
                    last.then_inc(on.used, 1)

            norm_transposes(1)
            open_banks(range(4, 8), 512)

            def gate_up(s, bank, moving, n):
                w = ring_slot(s)[:, 0:2 * D].rearrange("p (g k c) -> p g k c", g=2, k=KD)
                for g in range(2):
                    for k in range(KD):
                        last = mm(ps[:, bank, g * S:g * S + n], w[:, g, k, :], moving[:, k, :], k == 0, k == KD - 1)
                last.then_inc(on.gu_ready, 1)

            def dense_down(s, c):
                w = ring_slot(s)[:, 2 * D:3 * D]
                for b in range(TB):
                    for h in range(2):
                        last = mm(ps[:, 4 + 2 * b + h, :], hid[:, c % 2, b * P:(b + 1) * P],
                                  w[:, h * 512:(h + 1) * 512], False, False)
                last.then_inc(on.used, 1)

            with pe.Fori(0, HALF) as turn:
                for c in range(NS):
                    s = (FFN0 + c) % NS
                    pe.wait_ge(landed[s], turn * 16 + 16 * nth_load("ffn", c))
                    gate_up(s, c % 2, hT, S)
                    if c:
                        pe.wait_ge(on.hid_ready, turn * NS + c)
                        dense_down((FFN0 + c - 1) % NS, c - 1)
                pe.wait_ge(on.hid_ready, turn * NS + NS)
                dense_down((FFN0 + NS - 1) % NS, NS - 1)

            norm_transposes(2)
            for g in range(NIN):
                weights(pe, "qkv", g)
                w = item("qkv", g)[:, :].rearrange("p (k c) -> p k c", k=KD)
                n = CG if g < NIN - 1 else QKV - CG * (NIN - 1)
                for b in range(TB):
                    if g in (2, 3):
                        pe.wait_ge(on.rope_done, TB * (g - 2) + b + 1)
                    elif g in (4, 5):
                        pe.wait_ge(on.v_done, TB * (g - 4) + b + 1)
                    elif g == 6:
                        pe.wait_ge(on.rope_done, 2 * TB + b + 1)
                    for k in range(KD):
                        last = mm(ps[:, (2 * g + b) % 4, 0:n], hT[:, k, b * P:(b + 1) * P], w[:, k, 0:n],
                                  k == 0, k == KD - 1)
                        if g and b == k == 0:
                            last.then_inc(on.used, 1)
                    last.then_inc(on.qkv_ps, 1)

            for w in range(2):
                for b in range(TB):
                    pe.wait_ge(on.twice_done, 2 * w + b + 1)
                    for g in range(G):
                        last = flip(ps[:, 4 + 2 * w + b, g * P:(g + 1) * P],
                                    twice[:, w, b, g, :, :].rearrange("p i d -> p (i d)"))
                        if w == b == g == 0:
                            last.then_inc(on.used, 1)
                    last.then_inc(on.cT_ps, 1)
            pe.wait_ge(on.rope_done, 5 * TB)
            pe.wait_ge(on.gates_done, TB)
            for r in range(2):
                for a in range(2):
                    for b in range(TB):
                        c0 = (1 + r) * 256 + a * P
                        last = flip(ps[:, r, a * S + b * P:a * S + (b + 1) * P], k_t[:, b, c0:c0 + P])
                last.then_inc(on.kT_ps, 1)
            for i in range(4):
                if i >= 2:
                    pe.wait_ge(on.cT_done, i - 1)
                for n in (2 * i, 2 * i + 1):
                    for b in range(TB):
                        last = flip(ps[:, 2 + i, n % 2 * S + b * P:n % 2 * S + (b + 1) * P],
                                    q_t[:, b, n * P:(n + 1) * P])
                last.then_inc(on.qT_ps, 1)

            for i in range(3):
                weights(pe, "cmp", i)
            pe.wait_ge(on.cT_done, 4)
            for w in range(2):
                pe.wait_ge(on.flat_done, 2 * (w + 1))
                for m in range(2):
                    for i in range(16):
                        t = w * 16 + i
                        last = mm(ps[:, 6 + w, m * 60:(m + 1) * 60],
                                  item("cmp", t // 12)[:, t % 12 * HID + m * P:t % 12 * HID + (m + 1) * P],
                                  flat[:, w, i, :, :].rearrange("p g c -> p (g c)"), i == 0, i == 15)
                last.then_inc(on.ch_ps, 1)
            w2k = item("cmp", 2)[:, 2048:2304].rearrange("p (m d) -> p m d", m=2)
            w2v = item("cmp", 2)[:, 2304:2432].rearrange("p (m d) -> p m d", m=2)
            pe.wait_ge(on.ch_done, 1)
            pe.wait_ge(on.kT_done, 2)
            for m in range(2):
                last = mm(ps[:, 0, 0:60], w2k[:, m, :], hid_k[:, m * 60:(m + 1) * 60], m == 0, m == 1)
            last.then_inc(on.kc_ps, 1)
            pe.wait_ge(on.hid_v_done, 1)
            for g in range(G):
                for m in range(2):
                    last = mm(ps[:, 1, g * DH:(g + 1) * DH],
                              hid_v[:, m, g, :, :].rearrange("p j c -> p (j c)"), w2v[:, m, :], m == 0, m == 1)
            last.then_inc(on.vc_ps, 1)
            pe.wait_ge(on.kc_done, 1)
            pe.wait_ge(on.vc_done, 1)
            pe.wait_ge(on.qT_done, 4)

            def scores(u):
                b, n = divmod(u, KD)
                keys = P * (b + 1)
                if u >= 2:
                    pe.wait_ge(on.p_done, u - 1)
                for f in range(2):
                    for r in range(2):
                        last = mm(ps[:, 2 * (u % 2) + f, r * keys:(r + 1) * keys],
                                  qT[64 * f:64 * f + 64, n, b * P:(b + 1) * P],
                                  kT[64 * f:64 * f + 64, r, n // 4, 0:keys])
                last.then_inc(on.s_ps, 1)

            def transposes(u):
                b = u // KD
                pe.wait_ge(on.p_done, u + 1)
                if u:
                    pe.wait_ge(on.pTa_done, u)
                for f in range(2):
                    for r in range(2):
                        last = flip(ps[:, 4, (2 * f + r) * P:(2 * f + r + 1) * P], p_t[:, u % 2, f, r, 0:P])
                last.then_inc(on.pTa_ps, 1)
                if b:
                    if u > KD:
                        pe.wait_ge(on.pTv_done, u - KD)
                    for f in range(2):
                        for r in range(2):
                            last = flip(ps[:, 5, (2 * f + r) * P:(2 * f + r + 1) * P], p_t[:, u % 2, f, r, P:2 * P])
                    last.then_inc(on.pTv_ps, 1)

            def values(u):
                b, n = divmod(u, KD)
                pe.wait_ge(on.pTa_done, u + 1)
                if b:
                    pe.wait_ge(on.pTv_done, u - KD + 1)
                if u >= 2:
                    pe.wait_ge(on.o_done, u - 1)
                for f in range(2):
                    for r in range(2):
                        for kb in range(b + 1):
                            last = mm(ps[:, 6 + u % 2, (2 * f + r) * 65:(2 * f + r + 1) * 65],
                                      pT[:, u % 2, f, r, kb * P:(kb + 1) * P],
                                      v65[:, kb, 4 * r + 2 * (n // 4) + f, :], kb == 0, kb == b)
                last.then_inc(on.o_ps, 1)

            for b in range(TB):
                if b:
                    pe.wait_ge(on.o_done, KD)
                for n in range(KD):
                    for f in range(2):
                        g = 2 * (n // 4) + f
                        last = mm(ps[:, 6 + f, n * NC:(n + 1) * NC], qT[64 * f:64 * f + 64, n, b * P:(b + 1) * P],
                                  kcT[64 * f:64 * f + 64, g * NC:(g + 1) * NC])
                        if b == n == f == 0:
                            last.then_inc(on.used, 3)
                last.then_inc(on.sc_ps, 1)
                scores(KD * b)
                pe.wait_ge(on.pc_done, b + 1)
                for i in range(4):
                    last = flip(ps[:, 7, i * P:(i + 1) * P],
                                pc_t[:, 4 * i:4 * i + 4, :].rearrange("p h c -> p (h c)"))
                last.then_inc(on.pcT_ps, 1)
                pe.wait_ge(on.pcT_done, b + 1)
                for i in range(4):
                    last = mm(ps[:, 6 + i // 2, i % 2 * 256:(i % 2 + 1) * 256], pcT[:, i, :],
                              vbd[:, i // 2, :, :].rearrange("p j d -> p (j d)"))
                last.then_inc(on.oc_ps, 1)
                for u in range(KD * b, KD * (b + 1)):
                    if u + 1 < KD * (b + 1):
                        scores(u + 1)
                    transposes(u)
                    if u == KD * b:
                        pe.wait_ge(on.oc_done, b + 1)
                    else:
                        values(u - 1)
                values(KD * (b + 1) - 1)

            pe.wait_ge(on.o_done, TB * KD)
            for b in range(TB):
                for i in range(2):
                    for k in range(4):
                        last = flip(ps[:, 2 * b + i, k * P:(k + 1) * P], o_t[:, b, (4 * i + k) * P:(4 * i + k + 1) * P])
                    last.then_inc(on.oT_ps, 1)
            pe.wait_ge(on.oTa_done, TB)
            pe.wait_ge(on.oTv_done, TB)
            for k in range(KD):
                weights(pe, "nout", k // 3)
                w = item("nout", k // 3)[:, k % 3 * D:(k % 3 + 1) * D]
                for b in range(TB):
                    for h in range(2):
                        last = mm(ps[:, 4 + 2 * b + h, :], oT[:, k, b * P:(b + 1) * P],
                                  w[:, h * 512:(h + 1) * 512], k == 0, k == KD - 1)
                if k % 3 == 2 or k == KD - 1:
                    last.then_inc(on.used, 1)

            norm_transposes(3)
            router = par[:, W_RT:W_RT + KD * E].rearrange("p (k e) -> p k e", k=KD)
            for b in range(TB):
                for k in range(KD):
                    last = mm(ps[:, 0, b * E:(b + 1) * E], hT[:, k, b * P:(b + 1) * P], router[:, k, :],
                              k == 0, k == KD - 1)
            last.then_inc(on.logit_ps, 1)
            pe.wait_ge(on.asg_done, 1)
            mm(ps[:, 1, 0:E], tri, asg[:, 0, :])
            mm(ps[:, 1, E:2 * E], ones, asg[:, 0, :], True, False)
            mm(ps[:, 1, E:2 * E], tri, asg[:, 1, :], False, True)
            mm(ps[:, 1, 2 * E:3 * E], ones, asg[:, 0, :], True, False)
            mm(ps[:, 1, 2 * E:3 * E], ones, asg[:, 1, :], False, True).then_inc(on.pos_ps, 1)

            def gather():
                for n in range(KD):
                    for b in range(TB):
                        last = mm(ps[:, 4 + n // 4, n % 4 * CAP:(n % 4 + 1) * CAP], hn[:, b, n * P:(n + 1) * P],
                                  sel[:, b, :], b == 0, b == TB - 1)
                last.then_inc(on.gathered, 1)

            def expert_down(s, c):
                w = ring_slot(s)[:, 2 * D:3 * D]
                for n in range(KD):
                    last = mm(ps[:, 2 + n // 4, n % 4 * CAP:(n % 4 + 1) * CAP], w[:, n * P:(n + 1) * P],
                              hid[:, c % 2, 0:CAP], False, False)
                last.then_inc(on.used, 1)

            def expert_pass(p):
                with pe.Fori(0, HALF) as turn:
                    for c in range(NS):
                        s = (FFN0 + c) % NS
                        if c == 0:
                            pe.wait_ge(on.xe_ready, p + 1)
                        pe.wait_ge(landed[s], p * (16 * HALF) + turn * 16 + 16 * (LOADS[s] + 1))
                        gate_up(s, c % 2, xeT, CAP)
                        if c:
                            pe.wait_ge(on.hid_ready, p * NCH + turn * NS + (NCH + c))
                            expert_down((FFN0 + c - 1) % NS, c - 1)
                    pe.wait_ge(on.hid_ready, p * NCH + turn * NS + (NCH + NS))
                    expert_down((FFN0 + NS - 1) % NS, NS - 1)
                pe.wait_ge(on.sel_ready, p + 2)
                gather()
                pe.wait_ge(on.selw_ready, p + 1)
                for b in range(TB):
                    last = flip(ps[0:CAP, 0, b * P:(b + 1) * P], selw[:, b, :])
                last.then_inc(on.wT_ps, 1)
                pe.wait_ge(on.yT_ready, p + 1)
                for n in range(KD):
                    last = flip(ps[0:CAP, 6 + n // 4, n % 4 * P:(n % 4 + 1) * P], yT[:, n, :])
                last.then_inc(on.y_ps, 1)
                pe.wait_ge(on.wT_ready, p + 1)
                pe.wait_ge(on.y_ready, p + 1)
                for b in range(TB):
                    bank = 6 if b == 0 else 2
                    for h in range(2):
                        last = mm(ps[:, bank + h, :], selwT[0:CAP, b * P:(b + 1) * P],
                                  y_t[0:CAP, h * 512:(h + 1) * 512])
                    last.then_inc(on.comb_ps, 1)
                pe.wait_ge(on.comb_done, p * TB + TB)
                open_banks((2, 3), 4 * CAP)

            pe.wait_ge(on.sel_ready, 1)
            gather()
            open_banks((2, 3), 4 * CAP)
            with pe.Fori(0, E) as p:
                expert_pass(p)
            pe.wait_ge(on.ov_ready, 1)
            further = pe.value_load(ovt[0:1, 0:1], min_val=0, max_val=MAXOV)
            with pe.If(further > 0):
                with pe.Fori(E, further + E) as p:
                    expert_pass(p)

        @block.scalar
        def _(act):
            def norm_part(n):
                for b in range(TB):
                    if n == 0:
                        act.wait_ge(on.x_in, 16)
                    elif n < 4:
                        act.wait_ge(on.x_done, 4 * (n - 1) + 2 * b + 2)
                    nc.scalar.activation(hn[:, b, :], xs[:, b, :], ACT.Square,
                                         accum_out=stat[:, b:b + 1]).then_inc(on.norm_sq, 1)
                for b in range(TB):
                    act.wait_ge(on.norm_ms, TB * n + b + 1)
                    nc.scalar.activation(stat[:, 4 + b:5 + b], stat[:, 2 + b:3 + b], ACT.Sqrt
                                         ).then_inc(on.norm_rms, 1)
                if n < 4:
                    for b in range(TB):
                        act.wait_ge(on.norm_tr, 4 * n + 2 * b + 1)
                        nc.scalar.copy(hT[:, 0:4, b * P:(b + 1) * P],
                                       ps[:, 4 + 2 * b, :].rearrange("p (k t) -> p k t", k=4)
                                       ).then_inc(on.norm_hTa, 1)

            def load_row(buf, r):
                act.dma_start(row[:, buf, :], rows[r:r + 1, :].to_broadcast([P, D])).then_inc(row_in[buf], 16)

            norm_part(0)
            act.wait_ge(on.lam_abs, 1)
            nc.scalar.activation(lam_t[1], lam_t[0], ACT.Exp, scale=-1.0).then_inc(on.lam_exp, 1)
            act.wait_ge(on.norm_hn, 2)
            load_row(0, 2)
            for j in range(RT):
                act.wait_ge(on.xr_ps, j + 1)
                if j >= 2:
                    act.wait_ge(on.conv_done, j - 1)
                nc.scalar.activation(xr_t[j % 2][:, CONV - 1:], ps[:, j % 4, 0:S], ACT.Identity,
                                     bias=par[:, W_BX + j:W_BX + j + 1]).then_inc(on.xr_sb, 1)
            act.wait_ge(on.lam_sp, 1)
            for j in range(RT):
                act.wait_ge(on.bd_ps, j + 1)
                nc.scalar.activation(r_t[j % 2], ps[:, 4 + j % 4, 0:S], ACT.Sigmoid,
                                     bias=par[:, W_BA + j:W_BA + j + 1]).then_inc(on.r_done, 1)
                nc.scalar.activation(u_t[:, j, :], ps[:, 4 + j % 4, S:2 * S], ACT.Sigmoid,
                                     bias=par[:, W_BI + j:W_BI + j + 1]).then_inc(on.ig_done, 1)
                act.wait_ge(on.r_done, j + 1)
                nc.scalar.activation(th_t[:, j, :], r_t[j % 2], ACT.Tanh,
                                     scale=lam_t[5][:, j:j + 1]).then_inc(on.th_done, 1)
            act.wait_ge(on.th_done, RT)
            nc.scalar.activation(gate_t, th_t, ACT.Sqrt, scale=4.0).then_inc(on.sqrt_done, 1)
            act.wait_ge(on.bias_done, 1)
            load_row(1, 3)
            act.wait_ge(on.sqrt_used, 1)
            for j in range(RT):
                act.wait_ge(on.gate_ps, j + 1)
                nc.scalar.activation(gate_t[:, j, :], ps[:, j % 4, 0:S], ACT.Gelu_apprx_tanh,
                                     bias=par[:, W_BG + j:W_BG + j + 1]).then_inc(on.gate_done, 1)

            norm_part(1)
            act.wait_ge(on.norm_hn, 4)
            load_row(0, 4)
            with act.Fori(0, HALF) as turn:
                for c in range(NS):
                    act.wait_ge(on.gu_ready, turn * NS + (c + 1))
                    nc.scalar.activation(act_g[:, c % 2, :], ps[:, c % 2, 0:S], ACT.Silu).then_inc(on.silu_done, 1)

            norm_part(2)
            act.wait_ge(on.norm_hn, 6)
            load_row(1, 5)
            for g in (2, 3):
                for b in range(TB):
                    act.wait_ge(on.qkv_ps, TB * g + b + 1)
                    o = ps[:, (2 * g + b) % 4, :]
                    if g == 2:
                        nc.scalar.copy(vc_t[:, b, :], o[:, 0:256])
                        nc.scalar.copy(v65[:, b, 0:2, 0:DH], o[:, 256:384].rearrange("p (h d) -> p h d", d=DH)
                                       ).then_inc(on.v_done, 1)
                    else:
                        nc.scalar.copy(v65[:, b, 2:8, 0:DH], o[:, 0:384].rearrange("p (h d) -> p h d", d=DH)
                                       ).then_inc(on.v_done, 1)
            for b in range(TB):
                act.wait_ge(on.rope_done, 4 * TB + b + 1)
                nc.scalar.activation(gates[:, b, :, :].rearrange("p r h -> p (r h)"),
                                     ps[:, (2 * 6 + b) % 4, 256:304], ACT.Sigmoid).then_inc(on.gates_done, 1)
            for r in range(2):
                act.wait_ge(on.kT_ps, r + 1)
                nc.scalar.copy(kT[:, r, :, :].rearrange("p a t -> p (a t)"), ps[:, r, :]).then_inc(on.kT_done, 1)
            for i in range(4):
                act.wait_ge(on.qT_ps, i + 1)
                nc.scalar.copy(qT[:, 2 * i:2 * i + 2, :].rearrange("p n t -> p (n t)"), ps[:, 2 + i, :]
                               ).then_inc(on.qT_done, 1)
            act.wait_ge(on.ch_ps, 1)
            nc.scalar.activation(hid_k, ps[:, 6, 0:120], ACT.Gelu_apprx_tanh).then_inc(on.ch_done, 1)
            act.wait_ge(on.ch_ps, 2)
            act.wait_ge(on.zero_set, 2)
            for m in range(2):
                last = nc.scalar.activation(hid_v[:, m, :, 0, 0:NC],
                                            ps[:, 7, m * 60:(m + 1) * 60].rearrange("p (g c) -> p g c", g=G),
                                            ACT.Gelu_apprx_tanh)
            last.then_inc(on.ch_done, 1)

            def probs(u):
                b, n = divmod(u, KD)
                keys = P * (b + 1)
                act.wait_ge(on.s_max, u + 1)
                if u >= 2:
                    if u - 2 < KD:
                        act.wait_ge(on.pTa_ps, u - 1)
                    else:
                        act.wait_ge(on.pTv_ps, u - 1 - KD)
                for f in range(2):
                    for r in range(2):
                        last = nc.scalar.activation(p_t[:, u % 2, f, r, 0:keys],
                                                    ps[:, 2 * (u % 2) + f, r * keys:(r + 1) * keys], ACT.Exp,
                                                    bias=mx[u % 2][:, 2 * f + r:2 * f + r + 1])
                last.then_inc(on.p_done, 1)

            def evacuate(u):
                act.wait_ge(on.pTa_ps, u + 1)
                nc.scalar.copy(pT[:, u % 2, :, :, 0:P].rearrange("p f r q -> p (f r) q"),
                               ps[:, 4, :].rearrange("p (h q) -> p h q", h=4)).then_inc(on.pTa_done, 1)

            for b in range(TB):
                act.wait_ge(on.sc_sub, b + 1)
                nc.scalar.activation(pc_t[:, :, 0:NC], pc_t[:, :, 0:NC], ACT.Exp).then_inc(on.pc_exp, 1)
                act.wait_ge(on.pcT_ps, b + 1)
                nc.scalar.copy(pcT.rearrange("p g t -> p (g t)"), ps[:, 7, :]).then_inc(on.pcT_done, 1)
                probs(KD * b)
                for u in range(KD * b, KD * (b + 1)):
                    if u + 1 < KD * (b + 1):
                        probs(u + 1)
                    evacuate(u)
            for b in range(TB):
                act.wait_ge(on.oT_ps, 2 * b + 1)
                nc.scalar.copy(oT[:, 0:4, b * P:(b + 1) * P], ps[:, 2 * b, :].rearrange("p (k t) -> p k t", k=4)
                               ).then_inc(on.oTa_done, 1)

            norm_part(3)
            act.wait_ge(on.top_diff, 1)
            nc.scalar.activation(ev, dv, ACT.Exp).then_inc(on.top_exp, 1)

            def gathered_copy(n):
                act.wait_ge(on.gathered, n)
                nc.scalar.copy(xeT.rearrange("p (i n) t -> p i (n t)", i=2), ps[:, 4:6, 0:4 * CAP]
                               ).then_inc(on.xe_ready, 1)

            def expert_pass(p):
                with act.Fori(0, HALF) as turn:
                    for c in range(NS):
                        act.wait_ge(on.gu_ready, p * NCH + turn * NS + (NCH + c + 1))
                        nc.scalar.activation(act_g[:, c % 2, 0:CAP], ps[:, c % 2, 0:CAP], ACT.Silu
                                             ).then_inc(on.silu_done, 1)
                act.wait_ge(on.used, p * NCH + (MOE_AT + NCH))
                nc.scalar.copy(yT.rearrange("p (i n) t -> p i (n t)", i=2), ps[:, 2:4, 0:4 * CAP]
                               ).then_inc(on.yT_ready, 1)
                gathered_copy(p + 2)

            gathered_copy(1)
            with act.Fori(0, E) as p:
                expert_pass(p)
            act.wait_ge(on.ov_ready, 1)
            further = act.value_load(ovt[0:1, 0:1], min_val=0, max_val=MAXOV)
            with act.If(further > 0):
                with act.Fori(E, further + E) as p:
                    expert_pass(p)
            act.wait_ge(on.comb_done, further * TB + E * TB)
            norm_part(4)
            for b in range(TB):
                act.wait_ge(on.norm_hn, 4 * TB + b + 1)
                act.dma_start(out[0, b * P:(b + 1) * P, :], hn[:, b, :]).then_inc(on.out_done, 16)
            act.wait_ge(on.out_done, 16 * TB)

        @block.gpsimd
        def _(pool):
            for w in range(2):
                for b in range(TB):
                    pool.wait_ge(on.v_done if w else on.rope_done, b + 1)
                    src = vc_t[:, b, :] if w else k_t[:, b, 0:G * DH]
                    nc.gpsimd.tensor_copy(twice[:, w, b, :, :, :],
                                          src.rearrange("p (g d) -> p g d", g=G).unsqueeze(2)
                                          .to_broadcast([P, G, 2, DH])).then_inc(on.twice_done, 1)
            pool.wait_ge(on.ch_done, 2)
            for m in range(2):
                last = nc.gpsimd.tensor_copy(hid_v[:, m, :, 1:4, :],
                                             hid_v[:, m, :, 0:1, :].to_broadcast([P, G, 3, 32]))
            last.then_inc(on.hid_v_done, 1)

        @block.vector
        def _(dve):
            v = nc.vector
            steps = [0]

            def then(ins):
                steps[0] += 1
                ins.then_inc(on.dve_step, 1)
                dve.wait_ge(on.dve_step, steps[0])

            def norm_part(n, buf, loads):
                for b in range(TB):
                    dve.wait_ge(on.norm_sq, TB * n + b + 1)
                    v.tensor_scalar(stat[:, 2 + b:3 + b], stat[:, b:b + 1], 1.0 / D, EPS, ALU.mult, ALU.add
                                    ).then_inc(on.norm_ms, 1)
                dve.wait_ge(row_in[buf], 16 * loads)
                for b in range(TB):
                    dve.wait_ge(on.norm_rms, TB * n + b + 1)
                    then(v.reciprocal(stat[:, 6 + b:7 + b], stat[:, 4 + b:5 + b]))
                    v.scalar_tensor_tensor(hn[:, b, :], xs[:, b, :], stat[:, 6 + b:7 + b], row[:, buf, :],
                                           ALU.mult, ALU.mult).then_inc(on.norm_hn, 1)
                if n < 4:
                    for b in range(TB):
                        dve.wait_ge(on.norm_tr, 4 * n + 2 * b + 2)
                        v.tensor_copy(hT[:, 4:8, b * P:(b + 1) * P],
                                      ps[:, 5 + 2 * b, :].rearrange("p (k t) -> p k t", k=4)
                                      ).then_inc(on.norm_hTv, 1)

            def residual(ready, n):
                dve.wait_ge(on.used, ready)
                for b in range(TB):
                    for h in range(2):
                        o = xs[:, b, h * 512:(h + 1) * 512]
                        v.tensor_tensor(o, o, ps[:, 4 + 2 * b + h, :], ALU.add).then_inc(on.x_done, 1)
                dve.wait_ge(on.x_done, n)

            v.memset(zer[:, :], 0.0)
            for i in range(2):
                last = v.memset(xr_t[i][:, 0:CONV - 1], 0.0)
            last.then_inc(on.zero_set, 1)
            lam = par[:, W_LAM:W_LAM + RT]
            dve.wait_ge(on.const_in, 32)
            then(v.tensor_scalar(lam_t[2], lam, -1.0, None, ALU.mult))
            v.tensor_tensor(lam_t[0], lam, lam_t[2], ALU.max).then_inc(on.lam_abs, 1)
            norm_part(0, 0, 1)
            dve.wait_ge(on.lam_exp, 1)
            then(v.tensor_scalar(lam_t[3], lam_t[1], 2.0, None, ALU.add))
            then(v.reciprocal(lam_t[3], lam_t[3]))
            then(v.tensor_tensor(lam_t[1], lam_t[1], lam_t[3], ALU.mult))
            then(v.tensor_tensor(lam_t[3], lam_t[1], lam_t[1], ALU.mult))
            then(v.tensor_scalar(lam_t[4], lam_t[3], 1.0 / 17, None, ALU.mult))
            for k in range(15, 1, -2):
                then(v.scalar_tensor_tensor(lam_t[4], lam_t[4], 1.0 / k, lam_t[3], ALU.add, ALU.mult))
            then(v.scalar_tensor_tensor(lam_t[4], lam_t[4], 1.0, lam_t[1], ALU.add, ALU.mult))
            then(v.tensor_scalar(lam_t[2], lam_t[2], 0.0, None, ALU.max))
            then(v.scalar_tensor_tensor(lam_t[5], lam_t[4], 2.0, lam_t[2], ALU.mult, ALU.add))
            v.tensor_scalar(lam_t[5], lam_t[5], LRU_C / 2, None, ALU.mult).then_inc(on.lam_sp, 1)

            for j in range(RT):
                dve.wait_ge(on.xr_sb, j + 1)
                then(v.tensor_scalar(xc_t[:, j, :], xr_t[j % 2][:, 0:S], par[:, W_CW + j:W_CW + j + 1],
                                     par[:, W_CB + j:W_CB + j + 1], ALU.mult, ALU.add))
                for k in range(1, CONV):
                    c = W_CW + k * RT + j
                    ins = v.scalar_tensor_tensor(xc_t[:, j, :], xr_t[j % 2][:, k:k + S], par[:, c:c + 1],
                                                 xc_t[:, j, :], ALU.mult, ALU.add)
                    if k < CONV - 1:
                        then(ins)
                ins.then_inc(on.conv_done, 1)
            dve.wait_ge(row_in[1], 16)
            for b in range(TB):
                last = v.tensor_tensor(xs[:, b, :], xs[:, b, :], row[:, 1, :], ALU.add)
            last.then_inc(on.bias_done, 1)
            for j in range(RT):
                dve.wait_ge(on.ig_done, j + 1)
                v.tensor_tensor(u_t[:, j, :], u_t[:, j, :], xc_t[:, j, :], ALU.mult).then_inc(on.u_done, 1)
            dve.wait_ge(on.th_done, RT)
            dve.wait_ge(on.u_done, RT)
            then(v.tensor_scalar(xc_t, th_t, 1.0, None, ALU.add))
            then(v.reciprocal(xc_t, xc_t))
            dve.wait_ge(on.sqrt_done, 1)
            then(v.tensor_tensor(gate_t, gate_t, xc_t, ALU.mult))
            then(v.memset(gate_t[:, :, 0:1], 1.0))
            v.tensor_tensor(u_t, u_t, gate_t, ALU.mult).then_inc(on.sqrt_used, 1)
            then(v.tensor_scalar(th_t, th_t, -1.0, 1.0, ALU.mult, ALU.add))
            then(v.tensor_tensor(th_t, th_t, xc_t, ALU.mult))
            dve.wait_ge(on.sqrt_used, 1)
            for j in range(RT):
                then(v.tensor_tensor_scan(xc_t[:, j, :], th_t[:, j, :], u_t[:, j, :], 0.0, ALU.mult, ALU.add))
                dve.wait_ge(on.gate_done, j + 1)
                v.tensor_tensor(xc_t[:, j, :], xc_t[:, j, :], gate_t[:, j, :], ALU.mult).then_inc(on.y_done, 1)
            residual(INDEX[("lout", 3)] + 1, 4)
            norm_part(1, 0, 2)

            with dve.Fori(0, HALF) as turn:
                for c in range(NS):
                    dve.wait_ge(on.silu_done, turn * NS + (c + 1))
                    v.tensor_tensor(hid[:, c % 2, :], act_g[:, c % 2, :], ps[:, c % 2, S:2 * S], ALU.mult
                                    ).then_inc(on.hid_ready, 1)
            residual(INDEX[("ffn", NCH - 1)] + 1, 8)
            v.memset(v65[:, :, :, DH:DH + 1], 1.0)
            v.memset(vbd, 0.0)
            v.memset(pc_t, 0.0)
            v.memset(hid_v, 0.0).then_inc(on.zero_set, 1)
            norm_part(2, 1, 2)

            n = 0
            for g in (0, 1, 4, 5, 6):
                for b in range(TB):
                    dve.wait_ge(on.qkv_ps, TB * g + b + 1)
                    nh = 6 if g < 6 else 4
                    o = ps[:, (2 * g + b) % 4, 0:nh * DH].rearrange("p (h d) -> p h d", d=DH)
                    cs, sn = (C_COS, C_SIN) if g < 2 else (C_COSQ, C_SINQ)
                    cs = con[:, cs + b * DH:cs + (b + 1) * DH].unsqueeze(1).to_broadcast([P, nh, DH])
                    sn = con[:, sn + b * DH:sn + (b + 1) * DH].unsqueeze(1).to_broadcast([P, nh, DH])
                    dst = k_t[:, b, g * CG:g * CG + nh * DH] if g < 2 else \
                        q_t[:, b, (g - 4) * CG:(g - 4) * CG + nh * DH]
                    ra, rb = rope_a[n % 2][:, 0:nh, :], rope_b[n % 2][:, 0:nh, :]
                    if n >= 2:
                        dve.wait_ge(on.rope_done, n - 1)
                    n += 1
                    v.tensor_tensor(ra, o, cs, ALU.mult)
                    v.tensor_tensor(rb[:, :, 0:32], o[:, :, 32:64], sn[:, :, 0:32], ALU.mult)
                    then(v.tensor_tensor(rb[:, :, 32:64], o[:, :, 0:32], sn[:, :, 32:64], ALU.mult))
                    v.tensor_tensor(dst.rearrange("p (h d) -> p h d", d=DH), ra, rb, ALU.add
                                    ).then_inc(on.rope_done, 1)
            for w in range(2):
                for b in range(TB):
                    dve.wait_ge(on.cT_ps, 2 * w + b + 1)
                    o = ps[:, 4 + 2 * w + b, :].rearrange("p (g t) -> p g t", g=G)
                    v.tensor_copy(kv2T[0:64, w, :, b * P:(b + 1) * P], o[0:64, :, :])
                    lo = 1 - b
                    ins = v.tensor_copy(kv2T[64:128, w, :, b * P + lo - 1:(b + 1) * P - 1], o[64:128, :, lo:P])
                    ins.then_inc(on.cT_done, 1)
            pe_c = par[:, W_PE:W_PE + 32].rearrange("p (w i) -> p w i", w=2)
            dve.wait_ge(on.cT_done, 4)
            for w in range(2):
                view = kv2T[:, w, :, :].rearrange("p g (c r two) -> p g c r two", r=8, two=2)
                for i in range(2):
                    for g in range(G):
                        ins = v.tensor_tensor(flat[:, w, 8 * i:8 * i + 8, g, :],
                                              view[:, g, i:i + NC, :, 0].rearrange("p c r -> p r c"),
                                              pe_c[:, w, 8 * i:8 * i + 8].unsqueeze(2).to_broadcast([P, 8, NC]),
                                              ALU.add)
                    ins.then_inc(on.flat_done, 1)
            dve.wait_ge(on.kc_ps, 1)
            v.tensor_copy(kcT, ps[:, 0, 0:60]).then_inc(on.kc_done, 1)
            dve.wait_ge(on.vc_ps, 1)
            o = ps[:, 1, 0:256].rearrange("p (a f d) -> p a f d", a=2, f=2)
            for j in range(4):
                last = v.tensor_copy(vbd[32 * j:32 * j + 32, :, j, :], o[32 * j:32 * j + 32, :, j % 2, :])
            last.then_inc(on.vc_done, 1)

            def scores_max(u):
                b, n = divmod(u, KD)
                keys = P * (b + 1)
                dve.wait_ge(on.s_ps, u + 1)
                sc = ps[:, 2 * (u % 2):2 * (u % 2) + 2, 0:2 * keys].rearrange("p f (r k) -> p f r k", r=2)
                diag = sc[:, :, :, keys - P:keys]
                then(v.tensor_tensor(diag, diag, causal.unsqueeze(1).unsqueeze(1).to_broadcast([P, 2, 2, P]), ALU.add))
                v.tensor_reduce(mx[u % 2].rearrange("p (f r) -> p f r", f=2), sc, AX, ALU.max, negate=True
                                ).then_inc(on.s_max, 1)

            def evacuate(u):
                if u >= KD:
                    dve.wait_ge(on.pTv_ps, u - KD + 1)
                    v.tensor_copy(pT[:, u % 2, :, :, P:2 * P].rearrange("p f r q -> p (f r) q"),
                                  ps[:, 5, :].rearrange("p (h q) -> p h q", h=4)).then_inc(on.pTv_done, 1)

            def merge(u):
                b, n = divmod(u, KD)
                dve.wait_ge(on.o_ps, u + 1)
                if u:
                    dve.wait_ge(on.o_done, u)
                o = ps[:, 6 + u % 2, 0:260].rearrange("p (f r d) -> p f r d", f=2, r=2)
                rcv = rc.rearrange("p (f r) -> p f r", f=2)
                then(v.reciprocal(rcv, o[:, :, :, DH]))
                then(v.tensor_tensor(rcv, rcv, gates[:, b, 1:3, 2 * n:2 * n + 2].rearrange("p r f -> p f r"), ALU.mult))
                then(v.tensor_tensor(o_rw, o[:, :, :, 0:DH], rcv.unsqueeze(3).to_broadcast([P, 2, 2, DH]), ALU.mult))
                then(v.tensor_tensor(o_w, o_rw[:, :, 0, :], o_rw[:, :, 1, :], ALU.add))
                v.tensor_tensor(o_t[:, b, n * P:(n + 1) * P], o_w.rearrange("p f d -> p (f d)"),
                                o_c[:, n * P:(n + 1) * P], ALU.add).then_inc(on.o_done, 1)

            for b in range(TB):
                dve.wait_ge(on.sc_ps, b + 1)
                sc = ps[:, 6:8, 0:KD * NC].rearrange("p f (n c) -> p f n c", c=NC)
                cm = con[:, C_CM + b * NC:C_CM + (b + 1) * NC]
                cv = con[:, C_CV + b * NC:C_CV + (b + 1) * NC]
                then(v.tensor_tensor(sc, sc, cm.unsqueeze(1).unsqueeze(1).to_broadcast([P, 2, KD, NC]), ALU.add))
                cmx_v = cmx.rearrange("p (f n) -> p f n", f=2)
                then(v.tensor_reduce(cmx_v, sc, AX, ALU.max))
                pc = pc_t[:, :, 0:NC]
                v.tensor_tensor(pc.rearrange("p (n f) c -> p f n c", f=2), sc,
                                cmx_v.unsqueeze(3).to_broadcast([P, 2, KD, NC]), ALU.subtract
                                ).then_inc(on.sc_sub, 1)
                dve.wait_ge(on.pc_exp, b + 1)
                v.tensor_tensor(pc, pc, cv.unsqueeze(1).to_broadcast([P, H, NC]), ALU.mult).then_inc(on.pc_done, 1)
                dve.wait_ge(on.pc_done, b + 1)
                then(v.tensor_reduce(csum, pc, AX, ALU.add))
                then(v.tensor_scalar(csum, csum, 1e-30, None, ALU.max))
                then(v.reciprocal(csum, csum))
                then(v.tensor_tensor(csum, csum, gates[:, b, 0, :], ALU.mult))
                scores_max(KD * b)
                dve.wait_ge(on.oc_ps, b + 1)
                for i in range(2):
                    last = v.tensor_tensor(o_c[:, 512 * i:512 * (i + 1)].rearrange("p (h d) -> p h d", d=DH),
                                           ps[:, 6 + i, :].rearrange("p (h d) -> p h d", d=DH),
                                           csum[:, 8 * i:8 * i + 8].unsqueeze(2).to_broadcast([P, 8, DH]), ALU.mult)
                last.then_inc(on.oc_done, 1)
                dve.wait_ge(on.oc_done, b + 1)
                for u in range(KD * b, KD * (b + 1)):
                    if u + 1 < KD * (b + 1):
                        scores_max(u + 1)
                    evacuate(u)
                    if u > KD * b:
                        merge(u - 1)
                merge(KD * (b + 1) - 1)
            for b in range(TB):
                dve.wait_ge(on.oT_ps, 2 * b + 2)
                v.tensor_copy(oT[:, 4:8, b * P:(b + 1) * P], ps[:, 2 * b + 1, :].rearrange("p (k t) -> p k t", k=4)
                              ).then_inc(on.oTv_done, 1)
            residual(INDEX[("nout", 2)] + 1, 12)
            norm_part(3, 0, 3)

            dve.wait_ge(on.logit_ps, 1)
            then(v.tensor_copy(lg, ps[:, 0, 0:2 * E].rearrange("p (b e) -> p b e", b=TB)))
            for b in range(TB):
                then(v.max(m8[:, b, :], lg[:, b, :]))
            for b in range(TB):
                then(v.max_index(topi[:, b, :], m8[:, b, :], lg[:, b, :]))
            then(v.tensor_copy(idx, topi[:, :, :]))
            v.tensor_tensor(dv, m8[:, :, 1], m8[:, :, 0], ALU.subtract).then_inc(on.top_diff, 1)
            for b in range(TB):
                v.tensor_scalar(oh1[:, b, :], iota8, idx[:, b, 0:1], None, ALU.is_equal)
                last = v.tensor_scalar(oh2[:, b, :], iota8, idx[:, b, 1:2], None, ALU.is_equal)
            then(last)
            v.tensor_tensor(asg, oh1, oh2, ALU.add).then_inc(on.asg_done, 1)
            dve.wait_ge(on.top_exp, 1)
            then(v.tensor_scalar(den, ev, 1.0, None, ALU.add))
            then(v.reciprocal(w1, den))
            then(v.tensor_tensor(w2, ev, w1, ALU.mult))
            then(v.tensor_tensor(oh1, oh1, w1.unsqueeze(2).to_broadcast([P, TB, E]), ALU.mult))
            then(v.tensor_tensor(oh2, oh2, w2.unsqueeze(2).to_broadcast([P, TB, E]), ALU.mult))
            then(v.memset(posp, -1.0))
            then(v.memset(wp, 0.0))
            then(v.tensor_tensor(wp[:, :, 0:E], oh1, oh2, ALU.add))
            dve.wait_ge(on.pos_ps, 1)
            place = ps[:, 1, 0:2 * E].rearrange("p (b e) -> p b e", b=TB)
            then(v.scalar_tensor_tensor(posp[:, :, 0:E], place, 1.0, asg, ALU.add, ALU.mult))
            then(v.tensor_scalar(posp[:, :, 0:E], posp[:, :, 0:E], -1.0, None, ALU.add))

            def select(p):
                for b in range(TB):
                    last = v.tensor_scalar(sel[:, b, :], iota, posp[:, b, bass.ds(p, 1)], None, ALU.is_equal)
                last.then_inc(on.sel_ready, 1)

            def select_weighted(p):
                for b in range(TB):
                    last = v.tensor_scalar(selw[:, b, :], iota, posp[:, b, bass.ds(p, 1)], wp[:, b, bass.ds(p, 1)],
                                           ALU.is_equal, ALU.mult)
                last.then_inc(on.selw_ready, 1)

            cnt = ps[:, 1, 2 * E:3 * E]
            v.tensor_scalar(ov, cnt, float(CAP), None, ALU.is_gt)
            then(v.tensor_scalar(ov2, cnt, float(2 * CAP), None, ALU.is_gt))
            select(0)
            then(v.tensor_tensor(ov, ov, ov2, ALU.add))
            then(v.tensor_tensor_scan(cum, ones[:, 0:E], ov, 0.0, ALU.mult, ALU.add))
            then(v.tensor_tensor(cex, cum, ov, ALU.subtract))
            then(v.tensor_tensor(cmp_t, cum.unsqueeze(1).to_broadcast([P, MAXOV, E]),
                                 iota5.unsqueeze(2).to_broadcast([P, MAXOV, E]), ALU.is_le))
            then(v.tensor_reduce(ek, cmp_t, AX, ALU.add))
            then(v.tensor_tensor(ohk, iota8.unsqueeze(1).to_broadcast([P, MAXOV, E]),
                                 ek.unsqueeze(2).to_broadcast([P, MAXOV, E]), ALU.is_equal))
            then(v.tensor_tensor(prod, ohk, cex.unsqueeze(1).to_broadcast([P, MAXOV, E]), ALU.mult))
            then(v.tensor_reduce(cxk, prod, AX, ALU.add))
            then(v.tensor_tensor(off, iota5, cxk, ALU.subtract))
            then(v.tensor_scalar(off, off, 1.0, float(CAP), ALU.add, ALU.mult))
            for b in range(TB):
                for table in (posp, wp):
                    then(v.tensor_tensor(prod, ohk, table[:, b, 0:E].unsqueeze(1).to_broadcast([P, MAXOV, E]),
                                         ALU.mult))
                    then(v.tensor_reduce(table[:, b, E:MAXP], prod, AX, ALU.add))
                then(v.tensor_tensor(posp[:, b, E:MAXP], posp[:, b, E:MAXP], off, ALU.subtract))
            then(v.tensor_scalar(ek, ek, float(E - 1), None, ALU.min))
            v.tensor_copy(ovt[:, 0:1], cum[:, E - 1:E])
            v.tensor_copy(ovt[:, 1:1 + MAXOV], ek).then_inc(on.ov_ready, 1)
            dve.wait_ge(on.ov_ready, 1)

            def expert_pass(p):
                dve.wait_ge(on.gathered, p + 1)
                select(p + 1)
                select_weighted(p)
                with dve.Fori(0, HALF) as turn:
                    for c in range(NS):
                        dve.wait_ge(on.silu_done, p * NCH + turn * NS + (NCH + c + 1))
                        v.tensor_tensor(hid[:, c % 2, 0:CAP], act_g[:, c % 2, 0:CAP], ps[:, c % 2, S:S + CAP],
                                        ALU.mult).then_inc(on.hid_ready, 1)
                dve.wait_ge(on.wT_ps, p + 1)
                v.tensor_copy(selwT[0:CAP, :], ps[0:CAP, 0, 0:S]).then_inc(on.wT_ready, 1)
                dve.wait_ge(on.y_ps, p + 1)
                v.tensor_copy(y_t[0:CAP, :].rearrange("p (i n) -> p i n", i=2), ps[0:CAP, 6:8, :]
                              ).then_inc(on.y_ready, 1)
                for b in range(TB):
                    bank = 6 if b == 0 else 2
                    dve.wait_ge(on.comb_ps, p * TB + (b + 1))
                    xv = xs[:, b, :].rearrange("p (i n) -> p i n", i=2)
                    v.tensor_tensor(xv, xv, ps[:, bank:bank + 2, :], ALU.add).then_inc(on.comb_done, 1)

            with dve.Fori(0, E) as p:
                expert_pass(p)
            further = dve.value_load(ovt[0:1, 0:1], min_val=0, max_val=MAXOV)
            with dve.If(further > 0):
                with dve.Fori(E, further + E) as p:
                    expert_pass(p)
            dve.wait_ge(on.comb_done, further * TB + E * TB)
            norm_part(4, 1, 3)


def constants():
    import numpy as np
    c = np.zeros((P, NCONST), np.float32)
    c[:, C_ID:C_ID + P] = np.eye(P)
    c[:, C_TRI:C_TRI + P] = np.triu(np.ones((P, P)), 1)
    c[:, C_ONE:C_ONE + P] = 1.0
    c[:, C_CAU:C_CAU + P] = np.triu(np.full((P, P), NEG), 1)
    half = DH // 2
    freqs = np.float32(10000.0) ** (-np.arange(half, dtype=np.float32) / np.float32(half))
    ang = np.arange(S, dtype=np.float32)[:, None] * freqs[None, :]
    cos = np.cos(ang.astype(np.float32)).astype(np.float32).reshape(TB, P, half)
    sin = np.sin(ang.astype(np.float32)).astype(np.float32).reshape(TB, P, half)
    scale = np.float32(DH ** -0.5)
    for b in range(TB):
        cc = np.concatenate([cos[b], cos[b]], 1)
        ss = np.concatenate([-sin[b], sin[b]], 1)
        c[:, C_COS + b * DH:C_COS + (b + 1) * DH] = cc
        c[:, C_SIN + b * DH:C_SIN + (b + 1) * DH] = ss
        c[:, C_COSQ + b * DH:C_COSQ + (b + 1) * DH] = cc * scale
        c[:, C_SINQ + b * DH:C_SINQ + (b + 1) * DH] = ss * scale
        t = b * P + np.arange(P)
        seen = (np.arange(NC) * CS + CB - 1)[None, :] <= t[:, None]
        c[:, C_CM + b * NC:C_CM + (b + 1) * NC] = np.where(seen, 0.0, NEG)
        c[:, C_CV + b * NC:C_CV + (b + 1) * NC] = seen
    c[:, C_IOTA:C_IOTA + CAP] = np.arange(CAP)
    return c


def head_order():
    return [(2 * (n // 4) + f) * HP + n % 4 for n in range(KD) for f in range(2)]


def lay_out(a):
    import numpy as np
    f = np.float32

    def cols(v):
        return v.reshape(RT, P).T

    def pack(tiles, n_items):
        n, _, w = tiles.shape
        per = SW // w
        o = np.zeros((n_items, P, SW), f)
        for i in range(n_items):
            t = tiles[i * per:(i + 1) * per]
            o[i, :, :t.shape[0] * w] = t.transpose(1, 0, 2).reshape(P, -1)
        return o

    w_in = a["lru_w_in"][0]
    w_in = np.concatenate([w_in[:, RNN:], w_in[:, :RNN]], 1)
    tiles = w_in.reshape(KD, P, 2 * RT, P).transpose(2, 1, 0, 3).reshape(2 * RT, P, D)
    lru = pack(tiles, 8)
    bd = []
    full = np.zeros((2, RNN, RNN), f)
    for w, name in enumerate(("lru_w_a", "lru_w_i")):
        for b in range(RNN // BW):
            full[w, b * BW:(b + 1) * BW, b * BW:(b + 1) * BW] = a[name][0, b]
    for j in range(RT):
        for w in range(2):
            bd += [full[w, i * P:(i + 1) * P, j * P:(j + 1) * P] for i, jj in PAIRS if jj == j]
    bd = pack(np.stack(bd), BD_ITEMS)
    lout = pack(a["lru_w_out"][0].reshape(RT, P, D), 4)

    def chunks(g, u, d):
        n = g.shape[0]
        o = np.empty((n, NCH, P, 3, D), f)
        for i, w in enumerate((g, u)):
            o[:, :, :, i, :] = w.reshape(n, KD, P, NCH, P).transpose(0, 3, 2, 1, 4).reshape(n, NCH, P, D)
        o[:, :, :, 2, :] = d.reshape(n, NCH, P, D)
        return o.reshape(n * NCH, P, SW)

    ffn = chunks(a["ffn_w_gate"], a["ffn_w_up"], a["ffn_w_down"])
    moe = chunks(a["moe_w_gate"][0], a["moe_w_up"][0], a["moe_w_down"][0])

    w = a["nsa_w_in"][0]
    ho = head_order()
    at = np.cumsum([0, H * DH] + [G * DH] * 6)
    q, kc, vc, ks, vs, kw, vw = [w[:, at[i]:at[i + 1]] for i in range(7)]
    gg = w[:, at[7]:].reshape(D, H, 3)
    q = q.reshape(D, H, DH)[:, ho].reshape(D, H * DH)
    gg = gg[:, ho].transpose(0, 2, 1).reshape(D, 3 * H)
    w = np.concatenate([kc, ks, kw, vc, vs, vw, q, gg, np.zeros((D, NIN * CG - QKV), f)], 1)
    qkv = w.reshape(KD, P, NIN, CG).transpose(2, 1, 0, 3).reshape(NIN, P, SW)
    cmp = pack(a["nsa_cmp_w1"][0].reshape(32, P, HID), 3)
    w2 = a["nsa_cmp_w2"][0].reshape(2, 2, P, DH)
    for m in range(2):
        cmp[2, :, 2048 + m * P:2048 + m * P + DH] = w2[0, m]
        cmp[2, :, 2048 + m * P + DH:2048 + (m + 1) * P] = w2[0, m]
        cmp[2, :, 2304 + m * DH:2304 + (m + 1) * DH] = w2[1, m]
    nout = a["nsa_w_out"][0].reshape(H, DH, D)[ho].reshape(KD, P, D)
    nout = pack(nout, 3)

    par = np.zeros((P, NPAR), f)
    par[:, W_BX:W_BX + RT] = cols(a["lru_b_in"][0, RNN:])
    par[:, W_BG:W_BG + RT] = cols(a["lru_b_in"][0, :RNN])
    for k in range(CONV):
        par[:, W_CW + k * RT:W_CW + (k + 1) * RT] = cols(a["lru_conv_w"][0, k])
    for at_, name in ((W_CB, "lru_conv_b"), (W_BA, "lru_b_a"), (W_BI, "lru_b_i"), (W_LAM, "lru_lambda")):
        par[:, at_:at_ + RT] = cols(a[name][0])
    par[:, W_PE:W_PE + 32] = a["nsa_cmp_pe"][0].reshape(2, 16, P).transpose(2, 0, 1).reshape(P, 32)
    par[:, W_RT:W_RT + KD * E] = a["moe_w_router"][0].reshape(KD, P, E).transpose(1, 0, 2).reshape(P, KD * E)
    rows = np.stack([a["norm_mix"][0], a["lru_b_out"][0], a["norm_ffn"][0], a["norm_mix"][1], a["norm_ffn"][1],
                     a["norm_final"]])
    return {"x": a["x"], "consts": constants(), "params": par, "rows": rows, "w_lru": lru, "w_bd": bd,
            "w_lout": lout, "w_ffn": ffn, "w_qkv": qkv, "w_cmp": cmp, "w_nout": nout, "w_moe": moe}


def kernel(**inputs):
    import numpy as np
    import concourse.bacc as bacc
    from concourse.bass_utils import run_bass_kernel_spmd as run

    nc = bacc.Bacc("TRN2", target_bir_lowering=False, num_devices=1, dynamic_dma_scratch_size=256)
    arrays, args = {}, []
    for name, v in lay_out({k: np.asarray(v) for k, v in inputs.items()}).items():
        v = np.ascontiguousarray(v)
        arrays[f"in_{name}"] = v
        args.append(nc.dram_tensor(f"in_{name}", v.shape, mybir.dt.from_np(v.dtype), kind="ExternalInput").ap())
    args.append(nc.dram_tensor("out_0", (1, S, D), F32, kind="ExternalOutput").ap())
    build(nc, *args)
    r = run(nc, [arrays], core_ids=[0])
    return r.results[0]["out_0"]
```

```python
from contextlib import ExitStack

import concourse.bass as bass
from concourse import mybir

F32 = mybir.dt.float32
F32R = mybir.dt.float32r
BF16 = mybir.dt.bfloat16
U32 = mybir.dt.uint32
I32 = mybir.dt.int32
ALU = mybir.AluOpType
ACT = mybir.ActivationFunctionType
AX = mybir.AxisListType.X

P = 128
D = 1024
KD = D // P
S = 256
TB = S // P
RNN = 1408
RT = RNN // P
LRU_C = 8.0
BW = 88
CONV = 4
FF = 3584
NCH = FF // P
E = 8
CAP = 96
MAXOV = 5
H, G, HP, DH = 16, 4, 4, 64
NC = 15
CB, CS = 32, 16
HID = 256
QKV = 3 * 2 * G * DH + H * DH + 3 * H
NIN = 7
CG = 384
EPS = 1e-6
MAXP = E + MAXOV
NEG = -1e30

NS = 7
SW = 3072
TURN = 2 * NS
HALF = NCH // TURN
SLOT_TURNS = NCH // NS

PAIRS = [(i, j) for j in range(RT) for i in range(RT)
         if any(b * BW < (i + 1) * P and (b + 1) * BW > i * P and b * BW < (j + 1) * P and (b + 1) * BW > j * P
                for b in range(RNN // BW))]
BD_TILES = 2 * len(PAIRS)
BD_ITEMS = -(-BD_TILES * P // SW)

C_ID, C_TRI, C_ONE, C_CAU = 0, 128, 256, 384
C_COS, C_SIN, C_COSQ, C_SINQ = 512, 640, 768, 896
C_CM, C_CV = 1024, 1024 + TB * NC
C_IOTA = C_CV + TB * NC
NCONST = C_IOTA + CAP
W_BX, W_BG, W_CW, W_CB, W_BA, W_BI, W_LAM = 0, RT, 2 * RT, 6 * RT, 7 * RT, 8 * RT, 9 * RT
W_PE = 10 * RT
W_RT = W_PE + 32
NPAR = W_RT + KD * E



LRU_ORDER = [("lru", 0), ("lru", 1), ("lru", 2), ("lru", 3)] + [("bd", i) for i in range(BD_ITEMS)] + \
            [("lru", 4), ("lru", 5), ("lru", 6), ("lru", 7)] + [("lout", i) for i in range(4)]
NSA_ORDER = [("qkv", i) for i in range(NIN)] + [("cmp", i) for i in range(3)] + [("nout", i) for i in range(3)]
STATIC_SLOTS = 5
SLOT = {it: n % STATIC_SLOTS for order in (LRU_ORDER, NSA_ORDER) for n, it in enumerate(order)}
SLOT.update({(kind, c): c % NS for kind in ("ffn", "moe") for c in range(NCH)})

SPLITS = [("lru", i) for i in range(8)] + [("lout", i) for i in range(4)] + [("ffn", c) for c in range(NCH)] + \
         [("qkv", i) for i in range(NIN)] + [("nout", i) for i in range(3)] + [("moe", 0), ("moe", 1)]
SPLIT = {it: q for q, it in enumerate(SPLITS)}
Q_LOUT, Q_FFN, Q_QKV, Q_NOUT, Q_MOE = [SPLIT[(kind, 0)] for kind in ("lout", "ffn", "qkv", "nout", "moe")]
AHEAD = 2
RAW = [("bd", i) for i in range(BD_ITEMS)] + [("cmp", i) for i in range(3)]


def nth_load(kind, i):
    loads = LRU_ORDER + [("ffn", c) for c in range(NCH)] + NSA_ORDER + [("moe", c) for c in range(NCH)]
    n = loads.index((kind, i))
    return sum(1 for it in loads[:n + 1] if SLOT[it] == SLOT[(kind, i)])


def predecessor(kind, i):
    loads = LRU_ORDER + [("ffn", c) for c in range(NCH)] + NSA_ORDER + [("moe", c) for c in range(NS)]
    n = loads.index((kind, i))
    before = [it for it in loads[:n] if SLOT[it] == SLOT[(kind, i)]]
    return before[-1] if before else None


def build(nc, x, consts, params, rows, w_lru, w_bd, w_lout, w_ffn, w_qkv, w_cmp, w_nout, w_moe, out):
    with ExitStack() as ctx:
        def sb(name, shape, dt=F32):
            return ctx.enter_context(nc.sbuf_tensor(name, shape, dt))

        ring = sb("ring", [P, NS * SW])
        wh = sb("wh", [P, 2, SW], F32R)
        wl = sb("wl", [P, 2, SW], F32R)
        work = sb("work", [P, 7168])
        xs = sb("xs", [P, TB, D])
        hn = sb("hn", [P, TB, D])
        hTh = sb("hTh", [P, KD, S], F32R)
        hTl = sb("hTl", [P, KD, S], F32R)
        con = sb("con", [P, NCONST])
        par = sb("par", [P, NPAR])
        row = sb("row", [P, 2, D])
        arena = sb("arena", [P, 1536])
        stat = sb("stat", [P, 16])
        zer = sb("zer", [P, 512], BF16)
        ah = sb("ah", [P, 4, S])
        act_g = ah[:, 0:2, :]
        hid = ah[:, 2:4, :]
        hidh = sb("hidh", [P, 2, S], F32R)
        hidl = sb("hidl", [P, 2, S], F32R)
        rt = sb("rt", [P, 360])
        ovt = sb("ovt", [P, 8], I32)
        topi = sb("topi", [P, TB, 8], U32)
        ps = ctx.enter_context(nc.psum_tensor("ps", [P, 8, 512], F32))

        ident = con[:, C_ID:C_ID + P]
        tri = con[:, C_TRI:C_TRI + P]
        ones = con[:, C_ONE:C_ONE + P]
        causal = con[:, C_CAU:C_CAU + P]

        def ring_slot(s):
            return ring[:, s * SW:(s + 1) * SW]

        def item(kind, i):
            return ring_slot(SLOT[(kind, i)])

        def by_tile(buf):
            return buf.rearrange("p (j t) -> p j t", t=S)

        xc_t = by_tile(work[:, 0:RT * S])
        gate_t = by_tile(work[:, RT * S:2 * RT * S])
        a_t = [by_tile(hn[:, :, :].rearrange("p b c -> p (b c)")), by_tile(work[:, 2 * RT * S:2 * RT * S + 3 * S])]
        th_t = by_tile(ring_slot(5)[:, 0:RT * S])
        u_t = by_tile(ring_slot(6)[:, 0:RT * S])
        xr_t = [arena[:, 260 * i:260 * i + CONV - 1 + S] for i in range(2)]
        groups = ((0, 8), (8, RT))

        def a_tile(j):
            return a_t[j // 8][:, j % 8, :]

        lam_t = [arena[:, 1040 + 16 * i:1040 + 16 * i + RT] for i in range(6)]

        kv2T = work[:, 0:2048].rearrange("p (w g t) -> p w g t", w=2, g=G)
        flat = work[:, 2048:3968].rearrange("p (w i g c) -> p w i g c", w=2, i=16, g=G)
        pT = work[:, 0:2048].rearrange("p (u k f r t) -> p u k f r t", u=2, k=TB, f=2, r=2)
        pcT = work[:, 2048:3072].rearrange("p (b i t) -> p b i t", b=TB, i=4)
        qT = work[:, 4096:6144].rearrange("p (n t) -> p n t", n=KD)
        kT = work[:, 6144:7168].rearrange("p (r a t) -> p r a t", r=2, a=2)
        k_t = ring_slot(5)[:, 0:TB * 768].rearrange("p (b c) -> p b c", b=TB)
        hid_c = ring_slot(5)[:, 0:512].rearrange("p (w c) -> p w c", w=2)
        hid_k = ring_slot(5)[:, 512:632]
        v_t = ring_slot(5)[:, 1536:2560].rearrange("p (b c) -> p b c", b=TB)
        vc_t = ring_slot(5)[:, 2560:3072].rearrange("p (b c) -> p b c", b=TB)
        twice = ring_slot(6)[:, 0:2048].rearrange("p (w b g i d) -> p w b g i d", w=2, b=TB, g=G, i=2)
        pc_t = ring_slot(6)[:, 0:1024].rearrange("p (b h c) -> p b h c", b=TB, h=H)
        vbd = ring_slot(6)[:, 2048:2560].rearrange("p (a j d) -> p a j d", a=2, j=4)
        gates = ring_slot(6)[:, 2560:2656].rearrange("p (b r h) -> p b r h", b=TB, r=3)
        kcT = ring_slot(6)[:, 2656:2716].rearrange("p (a f c) -> p a f c", a=2, f=2)
        hid_v = ah[:, :, :].rearrange("p a t -> p (a t)").rearrange("p (m g j c) -> p m g j c", m=2, g=G, j=4)
        q_t = hn
        p_t = hn[:, :, :].rearrange("p u (f r k) -> p u f r k", f=2, r=2)
        rope_a, rope_b = [[arena[:, 768 * i + c:768 * i + c + CG].rearrange("p (h d) -> p h d", d=DH)
                           for i in range(2)] for c in (0, CG)]
        mx = [rt[:, 8 * i:8 * i + 4] for i in range(2)]
        sums = [rt[:, 16 + 8 * i:20 + 8 * i] for i in range(2)]
        rc = [rt[:, 32 + 8 * i:36 + 8 * i] for i in range(2)]
        cmx = rt[:, 48:80]
        csum = rt[:, 80:112]

        hT3 = work[:, 0:2048].rearrange("p (k t) -> p k t", k=KD)
        sel = work[:, 2048:2048 + TB * CAP].rearrange("p (b s) -> p b s", b=TB)
        selw = work[:, 2304:2304 + TB * CAP].rearrange("p (b s) -> p b s", b=TB)
        selwT = work[:, 2560:2816]
        xeh, xel = [t[:, :, :].rearrange("p n t -> p (n t)")[:, 0:KD * CAP].rearrange("p (n t) -> p n t", n=KD)
                    for t in (hTh, hTl)]
        y_t = row[:, 0, :]
        lg = rt[:, 0:16].rearrange("p (b e) -> p b e", b=TB)
        m8 = rt[:, 16:32].rearrange("p (b e) -> p b e", b=TB)
        idx = rt[:, 32:48].rearrange("p (b e) -> p b e", b=TB)
        dv, ev, den, w1, w2 = [rt[:, 48 + 2 * i:50 + 2 * i] for i in range(5)]
        oh1, oh2, asg = [rt[:, 64 + 16 * i:80 + 16 * i].rearrange("p (b e) -> p b e", b=TB) for i in range(3)]
        posp = rt[:, 112:140].rearrange("p (b e) -> p b e", b=TB)
        wp = rt[:, 140:168].rearrange("p (b e) -> p b e", b=TB)
        ov, ov2, cum, cex = [rt[:, 168 + 8 * i:176 + 8 * i] for i in range(4)]
        cmp_t = rt[:, 200:240].rearrange("p (k e) -> p k e", e=E)
        ek, cxk, off = [rt[:, 240 + 8 * i:240 + 8 * i + MAXOV] for i in range(3)]
        ohk = rt[:, 264:304].rearrange("p (k e) -> p k e", e=E)
        prod = rt[:, 304:344].rearrange("p (k e) -> p k e", e=E)
        iota8 = con[:, C_IOTA:C_IOTA + E]
        iota5 = con[:, C_IOTA:C_IOTA + MAXOV]
        iota = con[:, C_IOTA:C_IOTA + CAP]

        def sem(name):
            return ctx.enter_context(nc.semaphore(name))

        class on:
            const_in = sem("const_in")
            out_done = sem("out_done")
            wh_done = sem("wh_done")
            wl_done = sem("wl_done")
            wh2_done = sem("wh2_done")
            wl2_done = sem("wl2_done")
            used = sem("used")
            raw_used = sem("raw_used")
            zero_set = sem("zero_set")
            norm_sq = sem("norm_sq")
            norm_ms = sem("norm_ms")
            norm_rms = sem("norm_rms")
            norm_hn = sem("norm_hn")
            norm_tr = sem("norm_tr")
            norm_hTa = sem("norm_hTa")
            norm_hTv = sem("norm_hTv")
            lam_abs = sem("lam_abs")
            lam_exp = sem("lam_exp")
            lam_sp = sem("lam_sp")
            xr_ps = sem("xr_ps")
            xr_sb = sem("xr_sb")
            conv_done = sem("conv_done")
            bd_ps = sem("bd_ps")
            r_done = sem("r_done")
            ig_done = sem("ig_done")
            th_done = sem("th_done")
            th_read = sem("th_read")
            a_done = sem("a_done")
            u_done = sem("u_done")
            sqrt_done = sem("sqrt_done")
            sqrt_used = sem("sqrt_used")
            scan_done = sem("scan_done")
            gate_ps = sem("gate_ps")
            gate_done = sem("gate_done")
            y_done = sem("y_done")
            yh_done = sem("yh_done")
            yl_done = sem("yl_done")
            y_used = sem("y_used")
            block0_ps = sem("block0_ps")
            bias_done = sem("bias_done")
            x_done = sem("x_done")
            gu_ready = sem("gu_ready")
            silu_done = sem("silu_done")
            hid_ready = sem("hid_ready")
            hidT_ps = sem("hidT_ps")
            hh_done = sem("hh_done")
            hl_done = sem("hl_done")
            qkv_ps = sem("qkv_ps")
            rope_done = sem("rope_done")
            v_done = sem("v_done")
            gates_done = sem("gates_done")
            twice_done = sem("twice_done")
            cT_ps = sem("cT_ps")
            cT_done = sem("cT_done")
            flat_done = sem("flat_done")
            ch_ps = sem("ch_ps")
            ch_done = sem("ch_done")
            chT_ps = sem("chT_ps")
            chT_done = sem("chT_done")
            kc_ps = sem("kc_ps")
            vc_ps = sem("vc_ps")
            kc_done = sem("kc_done")
            vc_done = sem("vc_done")
            kT_ps = sem("kT_ps")
            kT_done = sem("kT_done")
            qT_ps = sem("qT_ps")
            qT_done = sem("qT_done")
            sc_ps = sem("sc_ps")
            sc_sub = sem("sc_sub")
            pc_exp = sem("pc_exp")
            pc_done = sem("pc_done")
            pcT_ps = sem("pcT_ps")
            pcT_done = sem("pcT_done")
            s_ps = sem("s_ps")
            s_max = sem("s_max")
            p_exp = sem("p_exp")
            p_done = sem("p_done")
            pT_ps = sem("pT_ps")
            pTa_done = sem("pTa_done")
            pTv_done = sem("pTv_done")
            pv_done = sem("pv_done")
            oh_done = sem("oh_done")
            ol_done = sem("ol_done")
            logit_ps = sem("logit_ps")
            top_diff = sem("top_diff")
            top_exp = sem("top_exp")
            asg_done = sem("asg_done")
            pos_ps = sem("pos_ps")
            ov_ready = sem("ov_ready")
            sel_ready = sem("sel_ready")
            selw_ready = sem("selw_ready")
            gathered = sem("gathered")
            xeh_done = sem("xeh_done")
            xel_done = sem("xel_done")
            wT_ps = sem("wT_ps")
            wT_ready = sem("wT_ready")
            y_ready = sem("y_ready")
            comb_ps = sem("comb_ps")
            comb_done = sem("comb_done")
            dve_step = sem("dve_step")

        x_in = [ctx.enter_context(nc.semaphore(f"x_in{b}")) for b in range(TB)]
        landed = [ctx.enter_context(nc.semaphore(f"landed{s}")) for s in range(NS)]
        row_in = [ctx.enter_context(nc.semaphore(f"row_in{i}")) for i in range(2)]
        block = ctx.enter_context(nc.Block())

        def weights(eng, kind, i):
            eng.wait_ge(landed[SLOT[(kind, i)]], 16 * nth_load(kind, i))

        @block.sync
        def _(sp):
            xv = x.rearrange("a (b p) d -> p (a b) d", p=P)
            sources = {"lru": w_lru, "bd": w_bd, "lout": w_lout, "ffn": w_ffn, "qkv": w_qkv, "cmp": w_cmp,
                       "nout": w_nout, "moe": w_moe}

            def split(n):
                sp.wait_ge(on.wl_done, 2 * n)
                sp.wait_ge(on.wl2_done, n)

            def load(kind, i):
                before = predecessor(kind, i)
                if before in RAW:
                    sp.wait_ge(on.raw_used, RAW.index(before) + 1)
                elif before:
                    split(SPLIT[before] + 1)
                s = SLOT[(kind, i)]
                sp.dma_start(ring_slot(s), sources[kind][i]).then_inc(landed[s], 16)

            for b in range(TB):
                sp.dma_start(xs[:, b, :], xv[:, b, :]).then_inc(x_in[b], 16)
            sp.dma_start(con[:, :], consts).then_inc(on.const_in, 16)
            sp.dma_start(row[:, 0, :], rows[0:1, :].to_broadcast([P, D])).then_inc(row_in[0], 16)
            sp.dma_start(par[:, :], params).then_inc(on.const_in, 16)
            for n, (kind, i) in enumerate(LRU_ORDER):
                load(kind, i)
                if n == 3:
                    sp.dma_start(row[:, 1, :], rows[1:2, :].to_broadcast([P, D])).then_inc(row_in[1], 16)
            for c in range(NS):
                if c == STATIC_SLOTS:
                    sp.wait_ge(on.scan_done, RT)
                load("ffn", c)
            sp.wait_ge(on.wl_done, 2 * (Q_FFN + 1))
            with sp.Fori(1, SLOT_TURNS) as turn:
                for c in range(NS):
                    sp.wait_ge(on.wl2_done, turn * NS + (Q_FFN + c - NS + 1))
                    sp.dma_start(ring_slot(c), w_ffn[bass.ds(turn * NS + c, 1)].rearrange("a p n -> p (a n)")
                                 ).then_inc(landed[c], 16)
            for kind, i in NSA_ORDER:
                load(kind, i)
            for c in (0, 1, 3, 4, 5, 6, 2):
                if c == STATIC_SLOTS:
                    sp.wait_ge(on.ol_done, 2 * TB)
                load("moe", c)
            sp.wait_ge(on.wl_done, 2 * (Q_MOE + 1))
            with sp.Fori(1, E * SLOT_TURNS) as turn:
                for c in range(NS):
                    sp.wait_ge(on.wl2_done, turn * NS + (Q_MOE + c - NS + 1))
                    sp.dma_start(ring_slot(c), w_moe[bass.ds(turn * NS + c, 1)].rearrange("a p n -> p (a n)")
                                 ).then_inc(landed[c], 16)
            sp.wait_ge(on.ov_ready, 1)
            further = sp.value_load(ovt[0:1, 0:1], min_val=0, max_val=MAXOV)
            e0 = sp.value_load(ovt[0:1, 1:2], min_val=0, max_val=E - 1)
            for c in range(AHEAD):
                split(Q_MOE + E * NCH + c - NS + 1)
                sp.dma_start(ring_slot(c), w_moe[bass.ds(e0 * NCH + c, 1)].rearrange("a p n -> p (a n)")
                             ).then_inc(landed[c], 16)
            with sp.If(further > 0):
                with sp.Fori(0, further) as k:
                    e = sp.value_load(ovt[0:1, bass.ds(k + 1, 1)], min_val=0, max_val=E - 1)
                    after = sp.value_load(ovt[0:1, bass.ds(k + 2, 1)], min_val=0, max_val=E - 1)
                    for c in range(AHEAD, NCH + AHEAD):
                        s = c % NS
                        chunk = e * NCH + c if c < NCH else after * NCH + (c - NCH)
                        sp.wait_ge(on.wl2_done, k * NCH + (Q_MOE + E * NCH + c - NS + 1))
                        sp.dma_start(ring_slot(s), w_moe[bass.ds(chunk, 1)].rearrange("a p n -> p (a n)")
                                     ).then_inc(landed[s], 16)

        @block.tensor
        def _(pe):
            def mm(o, a, b, start=True, stop=True):
                return nc.tensor.matmul(o, a, b, start=start, stop=stop, skip_group_check=True)

            def mm3(o, ah_, al_, bh_, bl_, start=False, stop=False):
                first = mm(o, ah_, bh_, start, False)
                mm(o, ah_, bl_, False, False)
                return first, mm(o, al_, bh_, False, stop)

            def flip(o, a, n=P):
                return nc.tensor.transpose(o, a, ident[0:n, 0:n])

            def piece(q, i):
                if i < 2:
                    pe.wait_ge(on.wl_done, 2 * q + i + 1)
                else:
                    pe.wait_ge(on.wl2_done, q + 1)

            def keep_warm(n, bank, fresh=True):
                for _ in range(n):
                    mm(ps[:, bank, :], zer[:, 0:P], zer[:, :], fresh, False)

            def norm_transposes(n):
                for b in range(TB):
                    pe.wait_ge(on.norm_hn, TB * n + b + 1)
                    for q in range(2):
                        for k in range(4):
                            last = flip(ps[:, 2 * b + q, k * P:(k + 1) * P],
                                        hn[:, b, (4 * q + k) * P:(4 * q + k + 1) * P])
                        last.then_inc(on.norm_tr, 1)
                keep_warm(6, 7, False)
                if n < 3:
                    pe.wait_ge(on.norm_hTv, 4 * (n + 1))
                else:
                    pe.wait_ge(on.norm_hTa, 4 * n + 2)
                    pe.wait_ge(on.norm_hTv, 4 * n + 2)

            def open_banks(banks, n, rows_=P):
                for k in banks:
                    last = mm(ps[0:rows_, k, 0:n], zer[:, 0:rows_], zer[:, 0:n])
                return last

            pe.wait_ge(on.zero_set, 1)
            keep_warm(30, 7)
            pe.wait_ge(on.const_in, 32)
            norm_transposes(0)

            def lru_tile(t, bank):
                q = t // 3
                piece(q, t % 3)
                wv, lv = [w[:, q % 2, t % 3 * D:(t % 3 + 1) * D].rearrange("p (k c) -> p k c", k=KD)
                          for w in (wh, wl)]
                for k in range(KD):
                    first, last = mm3(ps[:, bank, 0:S], wv[:, k, :], lv[:, k, :], hTh[:, k, :], hTl[:, k, :],
                                      k == 0, k == KD - 1)
                    if k == 0 and t and t % 3 == 0:
                        first.then_inc(on.used, 1)
                    if k == 0 and t == RT:
                        first.then_inc(on.raw_used, 1)
                return last

            for j in range(RT):
                if j >= 4:
                    pe.wait_ge(on.xr_sb, j - 3)
                lru_tile(j, j % 4).then_inc(on.xr_ps, 1)
            t = 0
            for j in range(RT):
                near = [i for i, jj in PAIRS if jj == j]
                pe.wait_ge(on.conv_done, max(near) + 1)
                if j >= 4:
                    pe.wait_ge(on.ig_done, j - 3)
                for w in range(2):
                    for i in near:
                        if t % (SW // P) == 0:
                            weights(pe, "bd", t // (SW // P))
                        o = t % (SW // P) * P
                        last = mm(ps[:, 4 + j % 4, w * S:(w + 1) * S],
                                  item("bd", t // (SW // P))[:, o:o + P], xc_t[:, i, :],
                                  i == near[0], i == near[-1])
                        if t and t % (SW // P) == 0:
                            last.then_inc(on.raw_used, 1)
                        t += 1
                last.then_inc(on.bd_ps, 1)
            for j in range(RT):
                if j >= 4:
                    pe.wait_ge(on.gate_done, j - 3)
                lru_tile(RT + j, j % 4).then_inc(on.gate_ps, 1)
            for k in range(RT):
                q = Q_LOUT + k // 3
                pe.wait_ge(on.yl_done, k + 1)
                piece(q, k % 3)
                c = k % 3 * D
                for b in range(TB):
                    for h in range(2):
                        first, last = mm3(ps[:, 4 + 2 * b + h, :], hidh[:, k % 2, b * P:(b + 1) * P],
                                          hidl[:, k % 2, b * P:(b + 1) * P],
                                          wh[:, q % 2, c + h * 512:c + (h + 1) * 512],
                                          wl[:, q % 2, c + h * 512:c + (h + 1) * 512], k == 0, k == RT - 1)
                        if b == h == 0 and k % 3 == 0:
                            first.then_inc(on.used, 1)
                        if b == 0 and h == 1 and k == RT - 1:
                            last.then_inc(on.block0_ps, 1)
                last.then_inc(on.y_used, 1)

            mm(ps[:, 0, 0:512], zer[:, 0:P], zer[:, :]).then_inc(on.used, 1)
            keep_warm(16, 3)
            pe.wait_ge(on.x_done, 4)
            open_banks(range(4, 8), 512)
            keep_warm(12, 3)
            norm_transposes(1)

            def dense_gate_up(par_, split_at):
                pe.wait_ge(on.wl_done, split_at)
                wv, lv = [w[:, par_, 0:2 * D].rearrange("p (k g c) -> p k g c", k=KD, g=2) for w in (wh, wl)]
                for g in range(2):
                    for k in range(KD):
                        _, last = mm3(ps[:, par_, g * S:(g + 1) * S], wv[:, k, g, :], lv[:, k, g, :],
                                      hTh[:, k, :], hTl[:, k, :], k == 0, k == KD - 1)
                last.then_inc(on.gu_ready, 1)

            def dense_down(par_, split_at, final=False):
                pe.wait_ge(on.wl2_done, split_at)
                for b in range(TB):
                    for h in range(2):
                        c = 2 * D + h * 512
                        _, last = mm3(ps[:, 4 + 2 * b + h, :], hidh[:, par_, b * P:(b + 1) * P],
                                      hidl[:, par_, b * P:(b + 1) * P],
                                      wh[:, par_, c:c + 512], wl[:, par_, c:c + 512])
                        if final and b == 0 and h == 1:
                            last.then_inc(on.block0_ps, 1)
                last.then_inc(on.used, 1)

            dense_gate_up(0, 2 * (Q_FFN + 1))
            with pe.Fori(0, 3) as r:
                for c in range(1, 9):
                    dense_gate_up(c % 2, r * 16 + 2 * (Q_FFN + c + 1))
                    pe.wait_ge(on.hl_done, r * 8 + c)
                    dense_down((c - 1) % 2, r * 8 + (Q_FFN + c))
            for c in range(NCH - 3, NCH):
                dense_gate_up(c % 2, 2 * (Q_FFN + c + 1))
                pe.wait_ge(on.hl_done, c)
                dense_down((c - 1) % 2, Q_FFN + c)
            pe.wait_ge(on.hl_done, NCH)
            dense_down(1, Q_FFN + NCH, True)

            keep_warm(30, 3)
            norm_transposes(2)

            def project(g):
                q = Q_QKV + g
                n = CG if g < NIN - 1 else QKV - CG * (NIN - 1)
                for b in range(TB):
                    if g in (2, 3):
                        pe.wait_ge(on.rope_done, TB * (g - 2) + b + 1)
                    elif g in (4, 5):
                        pe.wait_ge(on.v_done, TB * (g - 4) + b + 1)
                    elif g == 6:
                        pe.wait_ge(on.rope_done, 2 * TB + b + 1)
                    for k in range(KD):
                        if b == 0:
                            piece(q, ((k + 1) * CG - 1) // D)
                        c = k * CG
                        first, last = mm3(ps[:, (2 * g + b) % 4, 0:n], hTh[:, k, b * P:(b + 1) * P],
                                          hTl[:, k, b * P:(b + 1) * P], wh[:, q % 2, c:c + n],
                                          wl[:, q % 2, c:c + n], k == 0, k == KD - 1)
                        if g and b == k == 0:
                            first.then_inc(on.used, 1)
                    last.then_inc(on.qkv_ps, 1)

            def doubled_transposes(w):
                for b in range(TB):
                    pe.wait_ge(on.twice_done, 2 * w + b + 1)
                    for g in range(G):
                        last = flip(ps[:, 4 + 2 * w + b, g * P:(g + 1) * P],
                                    twice[:, w, b, g, :, :].rearrange("p i d -> p (i d)"))
                    last.then_inc(on.cT_ps, 1)

            for g in range(5):
                project(g)
            doubled_transposes(0)
            project(5)
            doubled_transposes(1)
            pe.wait_ge(on.cT_done, 2)
            for r in range(2):
                for a in range(2):
                    for b in range(TB):
                        c0 = (1 + r) * 256 + a * P
                        last = flip(ps[:, 4 + r, a * S + b * P:a * S + (b + 1) * P], k_t[:, b, c0:c0 + P])
                last.then_inc(on.kT_ps, 1)
            project(6)

            def compress(w):
                pe.wait_ge(on.flat_done, 2 * (w + 1))
                for i in range(16):
                    t = w * 16 + i
                    if t % 12 == 0:
                        weights(pe, "cmp", t // 12)
                    last = mm(ps[0:60, 6 + w, 0:HID], flat[:, w, i, :, :].rearrange("p g c -> p (g c)"),
                              item("cmp", t // 12)[:, t % 12 * HID:(t % 12 + 1) * HID], i == 0, i == 15)
                    if t == 0:
                        last.then_inc(on.used, 1)
                last.then_inc(on.ch_ps, 1)

            pe.wait_ge(on.cT_done, 4)
            compress(0)
            pe.wait_ge(on.rope_done, 5 * TB)
            for i in range(4):
                if i >= 2:
                    pe.wait_ge(on.kT_done, i - 1)
                for n in (2 * i, 2 * i + 1):
                    for b in range(TB):
                        last = flip(ps[:, 2 + i, n % 2 * S + b * P:n % 2 * S + (b + 1) * P],
                                    q_t[:, b, n * P:(n + 1) * P])
                last.then_inc(on.qT_ps, 1)
            compress(1)

            def scores(u):
                b, n = divmod(u, KD)
                keys = P * (b + 1)
                if u >= 2:
                    pe.wait_ge(on.p_exp, u - 1)
                for f in range(2):
                    for r in range(2):
                        last = mm(ps[:, 2 * ((u + 1) % 2) + f, r * keys:(r + 1) * keys],
                                  qT[64 * f:64 * f + 64, n, b * P:(b + 1) * P],
                                  kT[64 * f:64 * f + 64, r, n // 4, 0:keys])
                last.then_inc(on.s_ps, 1)

            pe.wait_ge(on.qT_done, 4)
            pe.wait_ge(on.kT_done, 2)
            scores(0)
            pe.wait_ge(on.gates_done, TB)
            for w in range(2):
                pe.wait_ge(on.ch_done, w + 1)
                for m in range(2):
                    last = flip(ps[:, w, m * 60:(m + 1) * 60], hid_c[0:60, w, m * P:(m + 1) * P], 60)
                last.then_inc(on.chT_ps, 1)
            w2k = item("cmp", 2)[:, 2048:2304].rearrange("p (m d) -> p m d", m=2)
            w2v = item("cmp", 2)[:, 2304:2432].rearrange("p (m d) -> p m d", m=2)
            keep_warm(6, 5)
            pe.wait_ge(on.chT_done, 1)
            for m in range(2):
                last = mm(ps[:, 6, 0:60], w2k[:, m, :], hid_k[:, m * 60:(m + 1) * 60], m == 0, m == 1)
            last.then_inc(on.kc_ps, 1)
            pe.wait_ge(on.chT_done, 2)
            for g in range(G):
                for m in range(2):
                    last = mm(ps[:, 7, g * DH:(g + 1) * DH],
                              hid_v[:, m, g, :, :].rearrange("p j c -> p (j c)"), w2v[:, m, :], m == 0, m == 1)
            last.then_inc(on.vc_ps, 1)
            scores(1)
            keep_warm(3, 5)
            pe.wait_ge(on.kc_done, 1)
            for b in range(TB):
                for n in range(KD):
                    c = (b * KD + n) * 2 * NC
                    last = mm(ps[:, 5, c:c + 2 * NC], qT[:, n, b * P:(b + 1) * P],
                              kcT[:, n // 4, :, :].rearrange("p f c -> p (f c)"))
                    if b == n == 0:
                        last.then_inc(on.raw_used, 3)
            last.then_inc(on.sc_ps, 1)

            def compressed_transposes(b):
                for i in range(4):
                    last = flip(ps[:, 5, i * P:(i + 1) * P],
                                pc_t[:, b, 4 * i:4 * i + 4, :].rearrange("p h c -> p (h c)"))
                last.then_inc(on.pcT_ps, 1)

            def transposes(u):
                b = u // KD
                pe.wait_ge(on.p_done, u + 1)
                if u:
                    pe.wait_ge(on.pTa_done, u)
                if u > KD:
                    pe.wait_ge(on.pTv_done, u - KD)
                for kb in range(b + 1):
                    for f in range(2):
                        for r in range(2):
                            last = flip(ps[:, 4 + kb, (2 * f + r) * P:(2 * f + r + 1) * P],
                                        p_t[:, u % 2, f, r, kb * P:(kb + 1) * P])
                last.then_inc(on.pT_ps, 1)

            def compressed_values(b, a):
                for n in range(4 * a, 4 * a + 4):
                    j = 2 * (n % 2)
                    mm(ps[:, 6 + a, n % 4 * P:(n % 4 + 1) * P],
                       vbd[:, a, j:j + 2, :].rearrange("p j d -> p (j d)"), pcT[:, b, n // 2, :], False, False)

            def values(u):
                b, n = divmod(u, KD)
                a = n // 4
                if u and n % 4 == 0:
                    if b:
                        pe.wait_ge(on.ol_done, a + 1)
                        open_banks((6 + a,), 512)
                        compressed_values(b, a)
                pe.wait_ge(on.pTa_done, u + 1)
                if b:
                    pe.wait_ge(on.pTv_done, u - KD + 1)
                for f in range(2):
                    for r in range(2):
                        for kb in range(b + 1):
                            c = (4 * r + 2 * a + f) * DH
                            last = mm(ps[64 * f:64 * f + 64, 6 + a, n % 4 * P:(n % 4 + 1) * P],
                                      v_t[:, kb, c:c + DH], pT[:, u % 2, kb, f, r, :], False, False)
                last.then_inc(on.pv_done, 1)

            pe.wait_ge(on.vc_done, 1)
            open_banks((6, 7), 512)
            for u in range(TB * KD):
                if u == 2:
                    pe.wait_ge(on.pc_done, 1)
                    compressed_transposes(0)
                elif u == 3:
                    pe.wait_ge(on.pcT_done, 1)
                    compressed_transposes(1)
                elif u == 4:
                    pe.wait_ge(on.pcT_done, TB)
                    for a in range(2):
                        compressed_values(0, a)
                if u + 2 < TB * KD:
                    scores(u + 2)
                if u < KD:
                    keep_warm(2, 7, False)
                transposes(u)
                if u:
                    values(u - 1)
            values(TB * KD - 1)

            for k in range(KD):
                q = Q_NOUT + k // 3
                pe.wait_ge(on.ol_done, 3 if k < 4 else 4)
                if k == 0:
                    pe.wait_ge(on.p_exp, TB * KD)
                piece(q, k % 3)
                c = k % 3 * D
                for b in range(TB):
                    for h in range(2):
                        _, last = mm3(ps[:, 2 * b + h, :], hTh[:, k, b * P:(b + 1) * P],
                                      hTl[:, k, b * P:(b + 1) * P], wh[:, q % 2, c + h * 512:c + (h + 1) * 512],
                                      wl[:, q % 2, c + h * 512:c + (h + 1) * 512], k == 0, k == KD - 1)
                        if b == 0 and h == 1 and k == KD - 1:
                            last.then_inc(on.block0_ps, 1)
                if k % 3 == 2 or k == KD - 1:
                    last.then_inc(on.used, 1)

            keep_warm(28, 7)
            norm_transposes(3)
            router = par[:, W_RT:W_RT + KD * E].rearrange("p (k e) -> p k e", k=KD)
            for b in range(TB):
                for k in range(KD):
                    last = mm(ps[:, 0, b * E:(b + 1) * E], hT3[:, k, b * P:(b + 1) * P], router[:, k, :],
                              k == 0, k == KD - 1)
            last.then_inc(on.logit_ps, 1)
            keep_warm(10, 7)
            pe.wait_ge(on.asg_done, 1)
            mm(ps[:, 1, 0:E], tri, asg[:, 0, :])
            mm(ps[:, 1, E:2 * E], ones, asg[:, 0, :], True, False)
            mm(ps[:, 1, E:2 * E], tri, asg[:, 1, :], False, True)
            mm(ps[:, 1, 2 * E:3 * E], ones, asg[:, 0, :], True, False)
            mm(ps[:, 1, 2 * E:3 * E], ones, asg[:, 1, :], False, True).then_inc(on.pos_ps, 1)

            def gather():
                for n in range(KD):
                    for b in range(TB):
                        last = mm(ps[:, 4 + n // 4, n % 4 * CAP:(n % 4 + 1) * CAP], hn[:, b, n * P:(n + 1) * P],
                                  sel[:, b, :], b == 0, b == TB - 1)
                last.then_inc(on.gathered, 1)

            def expert_gate_up(par_, split_at):
                for k in range(KD):
                    if k in (0, 4):
                        pe.wait_ge(on.wl_done, split_at + k // 4)
                    _, last = mm3(ps[0:CAP, par_, 0:2 * P], xeh[:, k, :], xel[:, k, :],
                                  wh[:, par_, k * 2 * P:(k + 1) * 2 * P], wl[:, par_, k * 2 * P:(k + 1) * 2 * P],
                                  k == 0, k == KD - 1)
                last.then_inc(on.gu_ready, 1)

            def hidden_transpose(par_, hid_at):
                pe.wait_ge(on.hid_ready, hid_at)
                flip(ps[:, par_, 2 * P:2 * P + CAP], hid[0:CAP, par_, 0:P], CAP).then_inc(on.hidT_ps, 1)

            def expert_down(par_, hid_at, split_at):
                pe.wait_ge(on.wl2_done, split_at)
                pe.wait_ge(on.hl_done, hid_at)
                for h in range(2):
                    c = 2 * D + h * 512
                    _, last = mm3(ps[0:CAP, 2 + h, :], hidh[:, par_, 0:CAP], hidl[:, par_, 0:CAP],
                                  wh[:, par_, c:c + 512], wl[:, par_, c:c + 512])
                last.then_inc(on.used, 1)

            def expert_pass(p):
                def step(c, more, more2):
                    expert_gate_up(c % 2, more2 + (2 * (Q_MOE + c) + 1))
                    expert_down((c - 1) % 2, more + (NCH + c), more + (Q_MOE + c))
                    hidden_transpose(c % 2, more + (NCH + c + 1))

                with pe.Fori(0, 2) as r:
                    for c in range(1, 13):
                        step(c, p * NCH + r * 12, p * (2 * NCH) + r * 24)
                for c in range(NCH - 3, NCH):
                    step(c, p * NCH, p * (2 * NCH))
                pe.wait_ge(on.sel_ready, p + 2)
                pe.wait_ge(on.comb_done, p * TB + 1)
                gather()
                expert_down(1, p * NCH + (NCH + NCH), p * NCH + (Q_MOE + NCH))
                pe.wait_ge(on.xel_done, p + 2)
                expert_gate_up(0, p * (2 * NCH) + (2 * (Q_MOE + NCH) + 1))
                pe.wait_ge(on.selw_ready, p + 1)
                for b in range(TB):
                    last = flip(ps[0:CAP, 1, b * P:(b + 1) * P], selw[:, b, :])
                last.then_inc(on.wT_ps, 1)
                pe.wait_ge(on.y_ready, p + 1)
                open_banks((2, 3), 512, CAP)
                hidden_transpose(0, p * NCH + (NCH + NCH + 1))
                pe.wait_ge(on.wT_ready, p + 1)
                for b in range(TB):
                    bank = 6 - 2 * b
                    for h in range(2):
                        last = mm(ps[:, bank + h, :], selwT[0:CAP, b * P:(b + 1) * P],
                                  y_t[0:CAP, h * 512:(h + 1) * 512])
                    last.then_inc(on.comb_ps, 1)

            keep_warm(8, 7)
            pe.wait_ge(on.sel_ready, 1)
            gather()
            open_banks((2, 3), 512, CAP)
            keep_warm(6, 7)
            pe.wait_ge(on.xel_done, 1)
            expert_gate_up(0, 2 * Q_MOE + 1)
            hidden_transpose(0, NCH + 1)
            with pe.Fori(0, E) as p:
                expert_pass(p)
            pe.wait_ge(on.ov_ready, 1)
            further = pe.value_load(ovt[0:1, 0:1], min_val=0, max_val=MAXOV)
            with pe.If(further > 0):
                with pe.Fori(E, further + E) as p:
                    expert_pass(p)

        @block.scalar
        def _(act):
            def high(q, i):
                kind, n = SPLITS[q]
                weights(act, kind, n)
                if q >= 2:
                    act.wait_ge(on.used, q - 1)
                    if i < 2:
                        act.wait_ge(on.wl_done, 2 * (q - 1))
                    else:
                        act.wait_ge(on.wl2_done, q - 1)
                c = slice(i * D, (i + 1) * D)
                nc.scalar.copy(wh[:, q % 2, c], item(kind, n)[:, c]
                               ).then_inc(on.wh_done if i < 2 else on.wh2_done, 1)

            def high_item(q):
                for i in range(3):
                    high(q, i)

            def norm_part(n, between=(), behind=(), further=None):
                if n == 0:
                    act.wait_ge(on.zero_set, 1)
                nc.scalar.activation(stat[:, 9:10], stat[:, 8:9], ACT.Sqrt)
                for b in range(TB):
                    if n == 0:
                        act.wait_ge(x_in[b], 16)
                    elif n < 4:
                        act.wait_ge(on.x_done, 4 * (n - 1) + 2 * b + 2)
                    else:
                        act.wait_ge(on.comb_done, further * TB + (E * TB + b))
                    nc.scalar.activation(hn[:, b, :], xs[:, b, :], ACT.Square,
                                         accum_out=stat[:, b:b + 1]).then_inc(on.norm_sq, 1)
                for b in range(TB):
                    act.wait_ge(on.norm_ms, TB * n + b + 1)
                    nc.scalar.activation(stat[:, 4 + b:5 + b], stat[:, 2 + b:3 + b], ACT.Sqrt
                                         ).then_inc(on.norm_rms, 1)
                for q, i in between:
                    high(q, i)
                if n < 3:
                    for i in range(4):
                        b, q = divmod(i, 2)
                        act.wait_ge(on.norm_tr, 4 * n + i + 1)
                        nc.scalar.copy(hTh[:, 4 * q:4 * q + 4, b * P:(b + 1) * P],
                                       ps[:, i, :].rearrange("p (k t) -> p k t", k=4)
                                       ).then_inc(on.norm_hTa, 1)
                elif n == 3:
                    for b in range(TB):
                        act.wait_ge(on.norm_tr, 4 * n + 2 * b + 1)
                        nc.scalar.copy(hT3[:, 0:4, b * P:(b + 1) * P],
                                       ps[:, 2 * b, :].rearrange("p (k t) -> p k t", k=4)
                                       ).then_inc(on.norm_hTa, 1)
                for q, i in behind:
                    high(q, i)

            def load_row(buf, r):
                act.dma_start(row[:, buf, :], rows[r:r + 1, :].to_broadcast([P, D])).then_inc(row_in[buf], 16)

            norm_part(0, (), [(0, i) for i in range(3)])
            act.wait_ge(on.lam_abs, 1)
            nc.scalar.activation(lam_t[1], lam_t[0], ACT.Exp, scale=-1.0).then_inc(on.lam_exp, 1)
            act.wait_ge(on.norm_hn, 2)
            load_row(0, 2)
            for j in range(RT):
                high((j + 3) // 3, (j + 3) % 3)
                act.wait_ge(on.xr_ps, j + 1)
                if j >= 2:
                    act.wait_ge(on.conv_done, j - 1)
                nc.scalar.activation(xr_t[j % 2][:, CONV - 1:], ps[:, j % 4, 0:S], ACT.Identity,
                                     bias=par[:, W_BX + j:W_BX + j + 1]).then_inc(on.xr_sb, 1)
            high(4, 2)
            def roots(group):
                j0, j1 = groups[group]
                act.wait_ge(on.th_read, j1)
                nc.scalar.activation(th_t[:, j0:j1, :], th_t[:, j0:j1, :], ACT.Sqrt).then_inc(on.sqrt_done, 1)

            act.wait_ge(on.lam_sp, 1)
            for j in range(RT):
                act.wait_ge(on.bd_ps, j + 1)
                nc.scalar.activation(a_tile(j), ps[:, 4 + j % 4, 0:S], ACT.Sigmoid,
                                     bias=par[:, W_BA + j:W_BA + j + 1]).then_inc(on.r_done, 1)
                nc.scalar.activation(u_t[:, j, :], ps[:, 4 + j % 4, S:2 * S], ACT.Sigmoid,
                                     bias=par[:, W_BI + j:W_BI + j + 1]).then_inc(on.ig_done, 1)
                act.wait_ge(on.r_done, j + 1)
                nc.scalar.activation(th_t[:, j, :], a_tile(j), ACT.Tanh,
                                     scale=lam_t[5][:, j:j + 1]).then_inc(on.th_done, 1)

            def y_high(k):
                act.wait_ge(on.y_done, k + 1)
                if k >= 2:
                    act.wait_ge(on.y_used, k - 1)
                nc.scalar.copy(hidh[:, k % 2, :], xc_t[:, k, :]).then_inc(on.yh_done, 1)

            for j in range(RT):
                act.wait_ge(on.gate_ps, j + 1)
                nc.scalar.activation(gate_t[:, j, :], ps[:, j % 4, 0:S], ACT.Gelu_apprx_tanh,
                                     bias=par[:, W_BG + j:W_BG + j + 1]).then_inc(on.gate_done, 1)
                t = j + 15
                if t < 24:
                    high(t // 3, t % 3)
                if j >= 9:
                    high(Q_LOUT, j - 9)
                if j == 2:
                    roots(0)
                    roots(1)
                if j in (3, 4):
                    y_high(j - 3)
            high(Q_LOUT, 2)
            for k in range(RT):
                if k + 2 < RT:
                    y_high(k + 2)
                if k + 3 < 12:
                    high(Q_LOUT + (k + 3) // 3, k % 3)
            act.wait_ge(on.bias_done, 1)
            load_row(1, 3)
            high_item(Q_FFN)

            norm_part(1, [(Q_FFN + 1, 0), (Q_FFN + 1, 1)])
            act.wait_ge(on.norm_hn, 4)
            load_row(0, 4)

            def copy_high(slot, par_, i):
                c = slice(i * D, (i + 1) * D)
                nc.scalar.copy(wh[:, par_, c], ring_slot(slot)[:, c]).then_inc(on.wh_done if i < 2 else on.wh2_done, 1)

            act.wait_ge(on.wl2_done, Q_FFN)
            with act.Fori(0, HALF) as turn:
                for c in range(TURN):
                    s1, s2 = (c + 1) % NS, (c + 2) % NS
                    act.wait_ge(on.gu_ready, turn * TURN + (c + 1))
                    nc.scalar.activation(act_g[:, c % 2, :], ps[:, c % 2, 0:S], ACT.Silu).then_inc(on.silu_done, 1)
                    act.wait_ge(landed[s2], turn * 32 + 16 * (nth_load("ffn", s2) + (c + 2) // NS))
                    copy_high(s2, c % 2, 0)
                    act.wait_ge(on.hid_ready, turn * TURN + (c + 1))
                    nc.scalar.copy(hidh[:, c % 2, :], hid[:, c % 2, :]).then_inc(on.hh_done, 1)
                    copy_high(s2, c % 2, 1)
                    act.wait_ge(on.used, turn * TURN + (Q_FFN + c))
                    copy_high(s1, (c + 1) % 2, 2)

            norm_part(2, [(Q_QKV + 1, 2)])
            act.wait_ge(on.norm_hn, 6)
            load_row(1, 5)
            for g in range(NIN):
                if g:
                    high_item(Q_QKV + 1 + g)
                for b in range(TB):
                    o = ps[:, (2 * g + b) % 4, :]
                    if g == 2:
                        act.wait_ge(on.qkv_ps, TB * g + b + 1)
                        nc.scalar.copy(vc_t[:, b, :], o[:, 0:256])
                        nc.scalar.copy(v_t[:, b, 0:128], o[:, 256:384]).then_inc(on.v_done, 1)
                    elif g == 3:
                        act.wait_ge(on.qkv_ps, TB * g + b + 1)
                        nc.scalar.copy(v_t[:, b, 128:512], o[:, 0:384]).then_inc(on.v_done, 1)
                if g == 5:
                    for r in range(2):
                        act.wait_ge(on.kT_ps, r + 1)
                        nc.scalar.copy(kT[:, r, :, :].rearrange("p a t -> p (a t)"), ps[:, 4 + r, :]
                                       ).then_inc(on.kT_done, 1)
            for b in range(TB):
                act.wait_ge(on.rope_done, 4 * TB + b + 1)
                nc.scalar.activation(gates[:, b, :, :].rearrange("p r h -> p (r h)"),
                                     ps[:, (2 * 6 + b) % 4, 256:304], ACT.Sigmoid).then_inc(on.gates_done, 1)
            high(Q_NOUT + 1, 0)
            for i in range(4):
                act.wait_ge(on.qT_ps, i + 1)
                nc.scalar.copy(qT[:, 2 * i:2 * i + 2, :].rearrange("p n t -> p (n t)"), ps[:, 2 + i, :]
                               ).then_inc(on.qT_done, 1)
            high(Q_NOUT + 1, 1)
            high(Q_NOUT + 1, 2)
            for w in range(2):
                act.wait_ge(on.ch_ps, w + 1)
                nc.scalar.activation(hid_c[0:60, w, :], ps[0:60, 6 + w, 0:HID], ACT.Gelu_apprx_tanh
                                     ).then_inc(on.ch_done, 1)

            def probs(u):
                b, n = divmod(u, KD)
                keys = P * (b + 1)
                act.wait_ge(on.s_max, u + 1)
                if u >= 2:
                    act.wait_ge(on.pT_ps, u - 1)
                for f in range(2):
                    for r in range(2):
                        i = 2 * f + r
                        last = nc.scalar.activation(p_t[:, u % 2, f, r, 0:keys],
                                                    ps[:, 2 * ((u + 1) % 2) + f, r * keys:(r + 1) * keys], ACT.Exp,
                                                    bias=mx[u % 2][:, i:i + 1], accum_out=sums[u % 2][:, i:i + 1])
                last.then_inc(on.p_exp, 1)

            def evacuate(u):
                act.wait_ge(on.pT_ps, u + 1)
                if u >= 2:
                    act.wait_ge(on.pv_done, u - 1)
                nc.scalar.copy(pT[:, u % 2, 0, :, :, :].rearrange("p f r t -> p (f r t)"), ps[:, 4, :]
                               ).then_inc(on.pTa_done, 1)

            def output_high(i):
                b, a = divmod(i, 2)
                act.wait_ge(on.pv_done, 4 * i + 4)
                nc.scalar.copy(hTh[:, 4 * a:4 * a + 4, b * P:(b + 1) * P],
                               ps[:, 6 + a, :].rearrange("p (n t) -> p n t", n=4)).then_inc(on.oh_done, 1)

            probs(0)
            probs(1)
            act.wait_ge(on.sc_sub, 1)
            nc.scalar.activation(pc_t[:, :, :, 0:NC].rearrange("p b h c -> p (b h) c"),
                                 pc_t[:, :, :, 0:NC].rearrange("p b h c -> p (b h) c"), ACT.Exp
                                 ).then_inc(on.pc_exp, 1)
            for u in range(TB * KD):
                if u in (2, 3):
                    b = u - 2
                    act.wait_ge(on.pcT_ps, b + 1)
                    nc.scalar.copy(pcT[:, b, :, :].rearrange("p i t -> p (i t)"), ps[:, 5, :]
                                   ).then_inc(on.pcT_done, 1)
                if u + 2 < TB * KD:
                    probs(u + 2)
                evacuate(u)
                if u and u % 4 == 0:
                    output_high(u // 4 - 1)
            output_high(3)
            high_item(Q_NOUT + 2)
            high_item(Q_MOE)

            norm_part(3, [(Q_MOE + 1, 0), (Q_MOE + 1, 1)])
            act.wait_ge(on.top_diff, 1)
            nc.scalar.activation(ev, dv, ACT.Exp).then_inc(on.top_exp, 1)

            def gathered_high(n):
                act.wait_ge(on.gathered, n)
                nc.scalar.copy(xeh.rearrange("p (i n) t -> p i (n t)", i=2), ps[:, 4:6, 0:4 * CAP]
                               ).then_inc(on.xeh_done, 1)

            def silu(par_, gu_at):
                act.wait_ge(on.gu_ready, gu_at)
                nc.scalar.activation(act_g[0:CAP, par_, 0:P], ps[0:CAP, par_, 0:P], ACT.Silu).then_inc(on.silu_done, 1)

            def expert_pass(p):
                for c in range(NCH):
                    s1, s2 = (c + 1) % NS, (c + 2) % NS
                    if c:
                        silu(c % 2, p * NCH + (NCH + c + 1))
                    act.wait_ge(landed[s2], p * (16 * SLOT_TURNS) + 16 * (nth_load("moe", s2) + (c + 2) // NS))
                    copy_high(s2, c % 2, 0)
                    act.wait_ge(on.hidT_ps, p * NCH + (c + 1))
                    nc.scalar.copy(hidh[:, c % 2, 0:CAP], ps[:, c % 2, 2 * P:2 * P + CAP]).then_inc(on.hh_done, 1)
                    copy_high(s2, c % 2, 1)
                    act.wait_ge(on.used, p * NCH + (Q_MOE + c))
                    copy_high(s1, (c + 1) % 2, 2)
                gathered_high(p + 2)
                act.wait_ge(on.used, p * NCH + (Q_MOE + NCH))
                nc.scalar.copy(y_t[0:CAP, :].rearrange("p (i n) -> p i n", i=2), ps[0:CAP, 2:4, :]
                               ).then_inc(on.y_ready, 1)
                silu(0, p * NCH + (NCH + NCH + 1))

            gathered_high(1)
            silu(0, NCH + 1)
            act.wait_ge(on.wl2_done, Q_MOE)
            with act.Fori(0, E) as p:
                expert_pass(p)
            act.wait_ge(on.ov_ready, 1)
            further = act.value_load(ovt[0:1, 0:1], min_val=0, max_val=MAXOV)
            with act.If(further > 0):
                with act.Fori(E, further + E) as p:
                    expert_pass(p)
            norm_part(4, further=further)
            for b in range(TB):
                act.wait_ge(on.norm_hn, 4 * TB + b + 1)
                act.dma_start(out[0, b * P:(b + 1) * P, :], hn[:, b, :]).then_inc(on.out_done, 16)
            act.wait_ge(on.out_done, 16 * TB)

        @block.gpsimd
        def _(pool):
            def less(s, par_):
                cols = slice(2 * D, 3 * D)
                nc.gpsimd.tensor_tensor(wl[:, par_, cols], ring_slot(s)[:, cols], wh[:, par_, cols].bitcast(F32),
                                        ALU.subtract).then_inc(on.wl2_done, 1)

            def low(q):
                pool.wait_ge(on.wh2_done, q + 1)
                less(SLOT[SPLITS[q]], q % 2)

            def subtract_low(c, split_at):
                pool.wait_ge(on.wh2_done, split_at)
                less(c % NS, c % 2)

            for q in range(Q_FFN + 1):
                low(q)
            with pool.Fori(0, HALF) as turn:
                for c in range(TURN):
                    subtract_low(c + 1, turn * TURN + (Q_FFN + c + 2))
            def double(w):
                for b in range(TB):
                    pool.wait_ge(on.v_done if w else on.rope_done, b + 1)
                    src = vc_t[:, b, :] if w else k_t[:, b, 0:G * DH]
                    nc.gpsimd.tensor_copy(twice[:, w, b, :, :, :],
                                          src.rearrange("p (g d) -> p g d", g=G).unsqueeze(2)
                                          .to_broadcast([P, G, 2, DH])).then_inc(on.twice_done, 1)

            for q in range(Q_QKV + 1, Q_MOE + 1):
                low(q)
                if q == Q_QKV + 2:
                    double(0)
                elif q == Q_QKV + 4:
                    double(1)

            def expert_pass(p):
                with pool.Fori(0, HALF) as turn:
                    for c in range(TURN):
                        subtract_low(c + 1, p * NCH + turn * TURN + (Q_MOE + c + 2))

            with pool.Fori(0, E) as p:
                expert_pass(p)
            pool.wait_ge(on.ov_ready, 1)
            further = pool.value_load(ovt[0:1, 0:1], min_val=0, max_val=MAXOV)
            with pool.If(further > 0):
                with pool.Fori(E, further + E) as p:
                    expert_pass(p)

        @block.vector
        def _(dve):
            v = nc.vector
            steps = [0]

            def then(ins):
                steps[0] += 1
                ins.then_inc(on.dve_step, 1)
                dve.wait_ge(on.dve_step, steps[0])

            def less(o, a, high_part):
                return v.tensor_tensor(o, a, high_part.bitcast(F32), ALU.subtract)

            def low(q, i):
                if i < 2:
                    dve.wait_ge(on.wh_done, 2 * q + i + 1)
                    c = slice(i * D, (i + 1) * D)
                    less(wl[:, q % 2, c], item(*SPLITS[q])[:, c], wh[:, q % 2, c]).then_inc(on.wl_done, 1)

            def low_item(q):
                for i in range(2):
                    low(q, i)

            def norm_part(n, buf, loads, between=(), behind=()):
                for b in range(TB):
                    dve.wait_ge(on.norm_sq, TB * n + b + 1)
                    v.tensor_scalar(stat[:, 2 + b:3 + b], stat[:, b:b + 1], 1.0 / D, EPS, ALU.mult, ALU.add
                                    ).then_inc(on.norm_ms, 1)
                dve.wait_ge(row_in[buf], 16 * loads)
                for b in range(TB):
                    dve.wait_ge(on.norm_rms, TB * n + b + 1)
                    then(v.reciprocal(stat[:, 6 + b:7 + b], stat[:, 4 + b:5 + b]))
                    v.scalar_tensor_tensor(hn[:, b, :], xs[:, b, :], stat[:, 6 + b:7 + b], row[:, buf, :],
                                           ALU.mult, ALU.mult).then_inc(on.norm_hn, 1)
                for q, i in between:
                    low(q, i)
                if n < 3:
                    for i in range(4):
                        b, q = divmod(i, 2)
                        dve.wait_ge(on.norm_hTa, 4 * n + i + 1)
                        c = slice(b * P, (b + 1) * P)
                        less(hTl[:, 4 * q:4 * q + 4, c], ps[:, i, :].rearrange("p (k t) -> p k t", k=4),
                             hTh[:, 4 * q:4 * q + 4, c]).then_inc(on.norm_hTv, 1)
                elif n == 3:
                    for b in range(TB):
                        dve.wait_ge(on.norm_tr, 4 * n + 2 * b + 2)
                        v.tensor_copy(hT3[:, 4:8, b * P:(b + 1) * P],
                                      ps[:, 1 + 2 * b, :].rearrange("p (k t) -> p k t", k=4)
                                      ).then_inc(on.norm_hTv, 1)
                for q, i in behind:
                    low(q, i)

            def residual(bank, n, done, count):
                for b in range(TB):
                    if b == 0:
                        dve.wait_ge(on.block0_ps, n // 4)
                    else:
                        dve.wait_ge(done, count)
                    for h in range(2):
                        o = xs[:, b, h * 512:(h + 1) * 512]
                        v.tensor_tensor(o, o, ps[:, bank + 2 * b + h, :], ALU.add).then_inc(on.x_done, 1)
                dve.wait_ge(on.x_done, n)

            v.memset(zer[:, :], 0.0)
            v.memset(stat[:, 8:9], 0.0)
            for i in range(2):
                last = v.memset(xr_t[i][:, 0:CONV - 1], 0.0)
            last.then_inc(on.zero_set, 1)
            norm_part(0, 0, 1, (), [(0, 0), (0, 1)])
            lam = par[:, W_LAM:W_LAM + RT]
            dve.wait_ge(on.const_in, 32)
            then(v.tensor_scalar(lam_t[2], lam, -1.0, None, ALU.mult))
            v.tensor_tensor(lam_t[0], lam, lam_t[2], ALU.max).then_inc(on.lam_abs, 1)

            def convolve(j):
                dve.wait_ge(on.xr_sb, j + 1)
                then(v.tensor_scalar(xc_t[:, j, :], xr_t[j % 2][:, 0:S], par[:, W_CW + j:W_CW + j + 1],
                                     par[:, W_CB + j:W_CB + j + 1], ALU.mult, ALU.add))
                for k in range(1, CONV):
                    c = W_CW + k * RT + j
                    ins = v.scalar_tensor_tensor(xc_t[:, j, :], xr_t[j % 2][:, k:k + S], par[:, c:c + 1],
                                                 xc_t[:, j, :], ALU.mult, ALU.add)
                    if k < CONV - 1:
                        then(ins)
                ins.then_inc(on.conv_done, 1)

            dve.wait_ge(on.lam_exp, 1)
            then(v.tensor_scalar(lam_t[3], lam_t[1], 2.0, None, ALU.add))
            then(v.reciprocal(lam_t[3], lam_t[3]))
            then(v.tensor_tensor(lam_t[1], lam_t[1], lam_t[3], ALU.mult))
            then(v.tensor_tensor(lam_t[3], lam_t[1], lam_t[1], ALU.mult))
            then(v.tensor_scalar(lam_t[4], lam_t[3], 1.0 / 17, None, ALU.mult))
            for k in range(15, 1, -2):
                then(v.scalar_tensor_tensor(lam_t[4], lam_t[4], 1.0 / k, lam_t[3], ALU.add, ALU.mult))
            then(v.scalar_tensor_tensor(lam_t[4], lam_t[4], 1.0, lam_t[1], ALU.add, ALU.mult))
            then(v.tensor_scalar(lam_t[2], lam_t[2], 0.0, None, ALU.max))
            then(v.scalar_tensor_tensor(lam_t[5], lam_t[4], 2.0, lam_t[2], ALU.mult, ALU.add))
            v.tensor_scalar(lam_t[5], lam_t[5], LRU_C / 2, None, ALU.mult).then_inc(on.lam_sp, 1)
            for j in range(RT):
                low((j + 3) // 3, (j + 3) % 3)
                convolve(j)

            def input_terms(group):
                j0, j1 = groups[group]
                dve.wait_ge(on.sqrt_done, group + 1)
                dve.wait_ge(on.a_done, j1)
                dve.wait_ge(on.u_done, j1)
                th, u, a = th_t[:, j0:j1, :], u_t[:, j0:j1, :], a_t[group][:, 0:j1 - j0, :]
                then(v.scalar_tensor_tensor(th, a, 1.0, th, ALU.add, ALU.mult))
                then(v.memset(th[:, :, 0:1], 1.0))
                v.tensor_tensor(u, u, th, ALU.mult).then_inc(on.sqrt_used, 1)

            for j in range(RT):
                dve.wait_ge(on.ig_done, j + 1)
                v.tensor_tensor(u_t[:, j, :], u_t[:, j, :], xc_t[:, j, :], ALU.mult).then_inc(on.u_done, 1)
                dve.wait_ge(on.th_done, j + 1)
                v.tensor_scalar(a_tile(j), th_t[:, j, :], 1.0, None, ALU.add).then_inc(on.th_read, 1)
                dve.wait_ge(on.th_read, j + 1)
                then(v.reciprocal(a_tile(j), a_tile(j)))
                v.tensor_scalar(a_tile(j), a_tile(j), 2.0, -1.0, ALU.mult, ALU.add).then_inc(on.a_done, 1)
            low(5, 0)
            low(5, 1)
            input_terms(0)
            dve.wait_ge(on.sqrt_used, 1)

            def y_tile(k):
                dve.wait_ge(on.scan_done, k + 1)
                dve.wait_ge(on.gate_done, k + 1)
                v.tensor_tensor(xc_t[:, k, :], xc_t[:, k, :], gate_t[:, k, :], ALU.mult).then_inc(on.y_done, 1)
                dve.wait_ge(on.yh_done, k + 1)
                less(hidl[:, k % 2, :], xc_t[:, k, :], hidh[:, k % 2, :]).then_inc(on.yl_done, 1)

            for j in range(RT):
                t = j + 15
                if 2 <= j and t < 24:
                    low(t // 3, t % 3)
                if j >= 9:
                    low(Q_LOUT, j - 9)
                if j == 6:
                    input_terms(1)
                    dve.wait_ge(on.sqrt_used, 2)
                v.tensor_tensor_scan(xc_t[:, j, :], a_tile(j), u_t[:, j, :], 0.0, ALU.mult, ALU.add
                                     ).then_inc(on.scan_done, 1)
                if j in (3, 4):
                    y_tile(j - 3)
            for k in range(RT):
                if k + 2 < RT:
                    y_tile(k + 2)
                if k + 3 < 12:
                    low(Q_LOUT + (k + 3) // 3, k % 3)
                if k == 5:
                    dve.wait_ge(row_in[1], 16)
                    for b in range(TB):
                        last = v.tensor_tensor(xs[:, b, :], xs[:, b, :], row[:, 1, :], ALU.add)
                    last.then_inc(on.bias_done, 1)
            low(Q_FFN, 0)
            low(Q_FFN, 1)
            dve.wait_ge(on.bias_done, 1)
            residual(4, 4, on.y_used, RT)
            norm_part(1, 0, 2, (), [(Q_FFN + 1, 0), (Q_FFN + 1, 1)])

            def subtract_low(slot, par_, i, split_at):
                dve.wait_ge(on.wh_done, split_at)
                c = slice(i * D, (i + 1) * D)
                less(wl[:, par_, c], ring_slot(slot)[:, c], wh[:, par_, c]).then_inc(on.wl_done, 1)

            with dve.Fori(0, HALF) as turn:
                for c in range(TURN):
                    s2 = (c + 2) % NS
                    at = turn * (2 * TURN)
                    dve.wait_ge(on.silu_done, turn * TURN + (c + 1))
                    v.tensor_tensor(hid[:, c % 2, :], act_g[:, c % 2, :], ps[:, c % 2, S:2 * S], ALU.mult
                                    ).then_inc(on.hid_ready, 1)
                    subtract_low(s2, c % 2, 0, at + (2 * (Q_FFN + c + 2) + 1))
                    dve.wait_ge(on.hh_done, turn * TURN + (c + 1))
                    less(hidl[:, c % 2, :], hid[:, c % 2, :], hidh[:, c % 2, :]).then_inc(on.hl_done, 1)
                    subtract_low(s2, c % 2, 1, at + (2 * (Q_FFN + c + 2) + 2))
            residual(4, 8, on.used, Q_QKV)
            v.memset(vbd, 0.0)
            v.memset(kcT, 0.0)
            v.memset(hid_v, 0.0).then_inc(on.zero_set, 1)
            norm_part(2, 1, 2)

            ropes = [0]

            def rotate(g):
                for b in range(TB):
                    dve.wait_ge(on.qkv_ps, TB * g + b + 1)
                    nh = 6 if g < 6 else 4
                    o = ps[:, (2 * g + b) % 4, 0:nh * DH].rearrange("p (h d) -> p h d", d=DH)
                    cs, sn = (C_COS, C_SIN) if g < 2 else (C_COSQ, C_SINQ)
                    cs = con[:, cs + b * DH:cs + (b + 1) * DH].unsqueeze(1).to_broadcast([P, nh, DH])
                    sn = con[:, sn + b * DH:sn + (b + 1) * DH].unsqueeze(1).to_broadcast([P, nh, DH])
                    dst = k_t[:, b, g * CG:g * CG + nh * DH] if g < 2 else \
                        q_t[:, b, (g - 4) * CG:(g - 4) * CG + nh * DH]
                    n = ropes[0]
                    ra, rb = rope_a[n % 2][:, 0:nh, :], rope_b[n % 2][:, 0:nh, :]
                    if n >= 2:
                        dve.wait_ge(on.rope_done, n - 1)
                    ropes[0] += 1
                    v.tensor_tensor(ra, o, cs, ALU.mult)
                    v.tensor_tensor(rb[:, :, 0:32], o[:, :, 32:64], sn[:, :, 0:32], ALU.mult)
                    then(v.tensor_tensor(rb[:, :, 32:64], o[:, :, 0:32], sn[:, :, 32:64], ALU.mult))
                    v.tensor_tensor(dst.rearrange("p (h d) -> p h d", d=DH), ra, rb, ALU.add
                                    ).then_inc(on.rope_done, 1)

            def doubled(w):
                for b in range(TB):
                    dve.wait_ge(on.cT_ps, 2 * w + b + 1)
                    o = ps[:, 4 + 2 * w + b, :].rearrange("p (g t) -> p g t", g=G)
                    v.tensor_copy(kv2T[0:64, w, :, b * P:(b + 1) * P], o[0:64, :, :])
                    lo = 1 - b
                    ins = v.tensor_copy(kv2T[64:128, w, :, b * P + lo - 1:(b + 1) * P - 1], o[64:128, :, lo:P])
                    ins.then_inc(on.cT_done, 1)

            pe_c = par[:, W_PE:W_PE + 32].rearrange("p (w i) -> p w i", w=2)

            def flatten(w):
                dve.wait_ge(on.cT_done, 2 * w + 2)
                view = kv2T[:, w, :, :].rearrange("p g (c r two) -> p g c r two", r=8, two=2)
                for i in range(2):
                    for g in range(G):
                        ins = v.tensor_tensor(flat[:, w, 8 * i:8 * i + 8, g, :],
                                              view[:, g, i:i + NC, :, 0].rearrange("p c r -> p r c"),
                                              pe_c[:, w, 8 * i:8 * i + 8].unsqueeze(2).to_broadcast([P, 8, NC]),
                                              ALU.add)
                    ins.then_inc(on.flat_done, 1)

            for g in range(NIN):
                if g:
                    low_item(Q_QKV + 1 + g)
                if g not in (2, 3):
                    rotate(g)
                if g == 4:
                    doubled(0)
                elif g == 5:
                    doubled(1)
                    flatten(0)
            flatten(1)
            v.memset(pc_t, 0.0).then_inc(on.zero_set, 1)
            low_item(Q_NOUT + 1)

            def scores_max(u):
                b, n = divmod(u, KD)
                keys = P * (b + 1)
                bank = 2 * ((u + 1) % 2)
                dve.wait_ge(on.s_ps, u + 1)
                sc = ps[:, bank:bank + 2, 0:2 * keys].rearrange("p f (r k) -> p f r k", r=2)
                diag = sc[:, :, :, keys - P:keys]
                then(v.tensor_tensor(diag, diag, causal.unsqueeze(1).unsqueeze(1).to_broadcast([P, 2, 2, P]), ALU.add))
                v.tensor_reduce(mx[u % 2].rearrange("p (f r) -> p f r", f=2), sc, AX, ALU.max, negate=True
                                ).then_inc(on.s_max, 1)

            def normalise(u):
                b, n = divmod(u, KD)
                keys = P * (b + 1)
                dve.wait_ge(on.p_exp, u + 1)
                then(v.reciprocal(rc[u % 2], sums[u % 2]))
                r4 = rc[u % 2].rearrange("p (f r) -> p f r", f=2)
                then(v.tensor_tensor(r4, r4, gates[:, b, 1:3, 2 * n:2 * n + 2].rearrange("p r f -> p f r"), ALU.mult))
                pv = p_t[:, u % 2, :, :, 0:keys]
                v.tensor_tensor(pv, pv, r4.unsqueeze(3).to_broadcast([P, 2, 2, keys]), ALU.mult
                                ).then_inc(on.p_done, 1)

            def evacuate(u):
                if u >= KD:
                    dve.wait_ge(on.pT_ps, u + 1)
                    dve.wait_ge(on.pv_done, u - 1)
                    v.tensor_copy(pT[:, u % 2, 1, :, :, :].rearrange("p f r t -> p (f r t)"), ps[:, 5, :]
                                  ).then_inc(on.pTv_done, 1)

            def output_low(i):
                b, a = divmod(i, 2)
                dve.wait_ge(on.oh_done, i + 1)
                c = slice(b * P, (b + 1) * P)
                less(hTl[:, 4 * a:4 * a + 4, c], ps[:, 6 + a, :].rearrange("p (n t) -> p n t", n=4),
                     hTh[:, 4 * a:4 * a + 4, c]).then_inc(on.ol_done, 1)

            scores_max(0)
            dve.wait_ge(on.chT_ps, 1)
            v.tensor_copy(hid_k, ps[:, 0, 0:120]).then_inc(on.chT_done, 1)
            dve.wait_ge(on.chT_ps, 2)
            for m in range(2):
                last = v.tensor_copy(hid_v[:, m, :, :, 0:NC],
                                     ps[:, 1, m * 60:(m + 1) * 60].rearrange("p (g c) -> p g c", g=G)
                                     .unsqueeze(2).to_broadcast([P, G, 4, NC]))
            last.then_inc(on.chT_done, 1)
            dve.wait_ge(on.kc_ps, 1)
            kc = ps[:, 6, 0:60].rearrange("p (a f c) -> p a f c", a=2, f=2)
            for f in range(2):
                last = v.tensor_copy(kcT[64 * f:64 * f + 64, :, f, :], kc[64 * f:64 * f + 64, :, f, :])
            last.then_inc(on.kc_done, 1)
            normalise(0)
            dve.wait_ge(on.vc_ps, 1)
            o = ps[:, 7, 0:256].rearrange("p (a f d) -> p a f d", a=2, f=2)
            for j in range(4):
                last = v.tensor_copy(vbd[32 * j:32 * j + 32, :, j, :], o[32 * j:32 * j + 32, :, j % 2, :])
            last.then_inc(on.vc_done, 1)
            scores_max(1)
            dve.wait_ge(on.sc_ps, 1)
            pc = pc_t[:, :, :, 0:NC]
            sc = ps[:, 5, 0:TB * H * NC].rearrange("p (b h c) -> p b h c", b=TB, h=H)
            cm = con[:, C_CM:C_CM + TB * NC].rearrange("p (b c) -> p b c", b=TB)
            then(v.tensor_tensor(pc, sc, cm.unsqueeze(2).to_broadcast([P, TB, H, NC]), ALU.add))
            cmx_v = cmx.rearrange("p (b h) -> p b h", b=TB)
            then(v.tensor_reduce(cmx_v, pc, AX, ALU.max))
            v.tensor_tensor(pc, pc, cmx_v.unsqueeze(3).to_broadcast([P, TB, H, NC]), ALU.subtract
                            ).then_inc(on.sc_sub, 1)
            normalise(1)
            scores_max(2)
            dve.wait_ge(on.pc_exp, 1)
            cv = con[:, C_CV:C_CV + TB * NC].rearrange("p (b c) -> p b c", b=TB)
            then(v.tensor_tensor(pc, pc, cv.unsqueeze(2).to_broadcast([P, TB, H, NC]), ALU.mult))
            csum_v = csum.rearrange("p (b h) -> p b h", b=TB)
            then(v.tensor_reduce(csum_v, pc, AX, ALU.add))
            then(v.tensor_scalar(csum, csum, 1e-30, None, ALU.max))
            then(v.reciprocal(csum, csum))
            then(v.tensor_tensor(csum_v, csum_v, gates[:, :, 0, :], ALU.mult))
            v.tensor_tensor(pc, pc, csum_v.unsqueeze(3).to_broadcast([P, TB, H, NC]), ALU.mult
                            ).then_inc(on.pc_done, 1)
            for u in range(TB * KD):
                if u and u + 2 < TB * KD:
                    scores_max(u + 2)
                if u and u + 1 < TB * KD:
                    normalise(u + 1)
                evacuate(u)
                if u and u % 4 == 0:
                    output_low(u // 4 - 1)
            output_low(3)
            low_item(Q_NOUT + 2)
            low_item(Q_MOE)
            residual(0, 12, on.used, Q_MOE)
            norm_part(3, 0, 3, (), [(Q_MOE + 1, 0), (Q_MOE + 1, 1)])

            dve.wait_ge(on.logit_ps, 1)
            then(v.tensor_copy(lg, ps[:, 0, 0:2 * E].rearrange("p (b e) -> p b e", b=TB)))
            for b in range(TB):
                then(v.max(m8[:, b, :], lg[:, b, :]))
            for b in range(TB):
                then(v.max_index(topi[:, b, :], m8[:, b, :], lg[:, b, :]))
            then(v.tensor_copy(idx, topi[:, :, :]))
            v.tensor_tensor(dv, m8[:, :, 1], m8[:, :, 0], ALU.subtract).then_inc(on.top_diff, 1)
            for b in range(TB):
                v.tensor_scalar(oh1[:, b, :], iota8, idx[:, b, 0:1], None, ALU.is_equal)
                last = v.tensor_scalar(oh2[:, b, :], iota8, idx[:, b, 1:2], None, ALU.is_equal)
            then(last)
            v.tensor_tensor(asg, oh1, oh2, ALU.add).then_inc(on.asg_done, 1)
            dve.wait_ge(on.top_exp, 1)
            then(v.tensor_scalar(den, ev, 1.0, None, ALU.add))
            then(v.reciprocal(w1, den))
            then(v.tensor_tensor(w2, ev, w1, ALU.mult))
            then(v.tensor_tensor(oh1, oh1, w1.unsqueeze(2).to_broadcast([P, TB, E]), ALU.mult))
            then(v.tensor_tensor(oh2, oh2, w2.unsqueeze(2).to_broadcast([P, TB, E]), ALU.mult))
            then(v.memset(posp, -1.0))
            then(v.memset(wp, 0.0))
            then(v.tensor_tensor(wp[:, :, 0:E], oh1, oh2, ALU.add))
            dve.wait_ge(on.pos_ps, 1)
            place = ps[:, 1, 0:2 * E].rearrange("p (b e) -> p b e", b=TB)
            then(v.scalar_tensor_tensor(posp[:, :, 0:E], place, 1.0, asg, ALU.add, ALU.mult))
            then(v.tensor_scalar(posp[:, :, 0:E], posp[:, :, 0:E], -1.0, None, ALU.add))

            def select(p):
                for b in range(TB):
                    last = v.tensor_scalar(sel[:, b, :], iota, posp[:, b, bass.ds(p, 1)], None, ALU.is_equal)
                last.then_inc(on.sel_ready, 1)

            def select_weighted(p):
                for b in range(TB):
                    last = v.tensor_scalar(selw[:, b, :], iota, posp[:, b, bass.ds(p, 1)], wp[:, b, bass.ds(p, 1)],
                                           ALU.is_equal, ALU.mult)
                last.then_inc(on.selw_ready, 1)

            cnt = ps[:, 1, 2 * E:3 * E]
            v.tensor_scalar(ov, cnt, float(CAP), None, ALU.is_gt)
            then(v.tensor_scalar(ov2, cnt, float(2 * CAP), None, ALU.is_gt))
            select(0)
            then(v.tensor_tensor(ov, ov, ov2, ALU.add))
            then(v.tensor_tensor_scan(cum, ones[:, 0:E], ov, 0.0, ALU.mult, ALU.add))
            then(v.tensor_tensor(cex, cum, ov, ALU.subtract))
            then(v.tensor_tensor(cmp_t, cum.unsqueeze(1).to_broadcast([P, MAXOV, E]),
                                 iota5.unsqueeze(2).to_broadcast([P, MAXOV, E]), ALU.is_le))
            then(v.tensor_reduce(ek, cmp_t, AX, ALU.add))
            then(v.tensor_tensor(ohk, iota8.unsqueeze(1).to_broadcast([P, MAXOV, E]),
                                 ek.unsqueeze(2).to_broadcast([P, MAXOV, E]), ALU.is_equal))
            then(v.tensor_tensor(prod, ohk, cex.unsqueeze(1).to_broadcast([P, MAXOV, E]), ALU.mult))
            then(v.tensor_reduce(cxk, prod, AX, ALU.add))
            then(v.tensor_tensor(off, iota5, cxk, ALU.subtract))
            then(v.tensor_scalar(off, off, 1.0, float(CAP), ALU.add, ALU.mult))
            for b in range(TB):
                for table in (posp, wp):
                    then(v.tensor_tensor(prod, ohk, table[:, b, 0:E].unsqueeze(1).to_broadcast([P, MAXOV, E]),
                                         ALU.mult))
                    then(v.tensor_reduce(table[:, b, E:MAXP], prod, AX, ALU.add))
                then(v.tensor_tensor(posp[:, b, E:MAXP], posp[:, b, E:MAXP], off, ALU.subtract))
            then(v.tensor_scalar(ek, ek, float(E - 1), None, ALU.min))
            v.tensor_copy(ovt[:, 0:1], cum[:, E - 1:E]).then_inc(on.comb_done, 1)
            v.tensor_copy(ovt[:, 1 + MAXOV:2 + MAXOV], ek[:, 0:1])
            v.tensor_copy(ovt[:, 1:1 + MAXOV], ek).then_inc(on.ov_ready, 1)
            dve.wait_ge(on.ov_ready, 1)

            def hidden(par_, silu_at):
                dve.wait_ge(on.silu_done, silu_at)
                v.tensor_tensor(hid[0:CAP, par_, 0:P], act_g[0:CAP, par_, 0:P], ps[0:CAP, par_, P:2 * P],
                                ALU.mult).then_inc(on.hid_ready, 1)

            def expert_pass(p):
                dve.wait_ge(on.gathered, p + 1)
                select(p + 1)
                select_weighted(p)
                for c in range(NCH):
                    if c:
                        hidden(c % 2, p * NCH + (NCH + c + 1))
                    s2 = (c + 2) % NS
                    subtract_low(s2, c % 2, 0, p * (2 * NCH) + (2 * (Q_MOE + c + 2) + 1))
                    dve.wait_ge(on.hh_done, p * NCH + (NCH + c + 1))
                    less(hidl[:, c % 2, 0:CAP], ps[:, c % 2, 2 * P:2 * P + CAP], hidh[:, c % 2, 0:CAP]
                         ).then_inc(on.hl_done, 1)
                    subtract_low(s2, c % 2, 1, p * (2 * NCH) + (2 * (Q_MOE + c + 2) + 2))
                gathered_low(p + 2)
                dve.wait_ge(on.wT_ps, p + 1)
                v.tensor_copy(selwT[0:CAP, :], ps[0:CAP, 1, 0:S]).then_inc(on.wT_ready, 1)
                hidden(0, p * NCH + (NCH + NCH + 1))
                for b in range(TB):
                    bank = 6 - 2 * b
                    dve.wait_ge(on.comb_ps, p * TB + (b + 1))
                    xv = xs[:, b, :].rearrange("p (i n) -> p i n", i=2)
                    v.tensor_tensor(xv, xv, ps[:, bank:bank + 2, :], ALU.add).then_inc(on.comb_done, 1)

            def gathered_low(n):
                dve.wait_ge(on.xeh_done, n)
                less(xel.rearrange("p (i n) t -> p i (n t)", i=2), ps[:, 4:6, 0:4 * CAP],
                     xeh.rearrange("p (i n) t -> p i (n t)", i=2)).then_inc(on.xel_done, 1)

            gathered_low(1)
            hidden(0, NCH + 1)
            with dve.Fori(0, E) as p:
                expert_pass(p)
            further = dve.value_load(ovt[0:1, 0:1], min_val=0, max_val=MAXOV)
            with dve.If(further > 0):
                with dve.Fori(E, further + E) as p:
                    expert_pass(p)
            dve.wait_ge(on.comb_done, further * TB + (E * TB + 1))
            norm_part(4, 1, 3)


def constants():
    import numpy as np
    c = np.zeros((P, NCONST), np.float32)
    c[:, C_ID:C_ID + P] = np.eye(P)
    c[:, C_TRI:C_TRI + P] = np.triu(np.ones((P, P)), 1)
    c[:, C_ONE:C_ONE + P] = 1.0
    c[:, C_CAU:C_CAU + P] = np.triu(np.full((P, P), NEG), 1)
    half = DH // 2
    freqs = np.float32(10000.0) ** (-np.arange(half, dtype=np.float32) / np.float32(half))
    ang = np.arange(S, dtype=np.float32)[:, None] * freqs[None, :]
    cos = np.cos(ang.astype(np.float32)).astype(np.float32).reshape(TB, P, half)
    sin = np.sin(ang.astype(np.float32)).astype(np.float32).reshape(TB, P, half)
    scale = np.float32(DH ** -0.5)
    for b in range(TB):
        cc = np.concatenate([cos[b], cos[b]], 1)
        ss = np.concatenate([-sin[b], sin[b]], 1)
        c[:, C_COS + b * DH:C_COS + (b + 1) * DH] = cc
        c[:, C_SIN + b * DH:C_SIN + (b + 1) * DH] = ss
        c[:, C_COSQ + b * DH:C_COSQ + (b + 1) * DH] = cc * scale
        c[:, C_SINQ + b * DH:C_SINQ + (b + 1) * DH] = ss * scale
        t = b * P + np.arange(P)
        seen = (np.arange(NC) * CS + CB - 1)[None, :] <= t[:, None]
        c[:, C_CM + b * NC:C_CM + (b + 1) * NC] = np.where(seen, 0.0, NEG)
        c[:, C_CV + b * NC:C_CV + (b + 1) * NC] = seen
    c[:, C_IOTA:C_IOTA + CAP] = np.arange(CAP)
    return c


def head_order():
    return [(2 * (n // 4) + f) * HP + n % 4 for n in range(KD) for f in range(2)]


def lay_out(a):
    import numpy as np
    f = np.float32

    def cols(v):
        return v.reshape(RT, P).T

    def pack(tiles, n_items):
        n, _, w = tiles.shape
        per = SW // w
        o = np.zeros((n_items, P, SW), f)
        for i in range(n_items):
            t = tiles[i * per:(i + 1) * per]
            o[i, :, :t.shape[0] * w] = t.transpose(1, 0, 2).reshape(P, -1)
        return o

    w_in = a["lru_w_in"][0]
    w_in = np.concatenate([w_in[:, RNN:], w_in[:, :RNN]], 1)
    tiles = w_in.reshape(KD, P, 2 * RT, P).transpose(2, 1, 0, 3).reshape(2 * RT, P, D)
    lru = pack(tiles, 8)
    bd = []
    full = np.zeros((2, RNN, RNN), f)
    for w, name in enumerate(("lru_w_a", "lru_w_i")):
        for b in range(RNN // BW):
            full[w, b * BW:(b + 1) * BW, b * BW:(b + 1) * BW] = a[name][0, b]
    for j in range(RT):
        for w in range(2):
            bd += [full[w, i * P:(i + 1) * P, j * P:(j + 1) * P] for i, jj in PAIRS if jj == j]
    bd = pack(np.stack(bd), BD_ITEMS)
    lout = pack(a["lru_w_out"][0].reshape(RT, P, D), 4)

    def chunks(g, u, d):
        n = g.shape[0]
        o = np.empty((n, NCH, P, SW), f)
        gu = o[:, :, :, 0:2 * D].reshape(n, NCH, P, KD, 2, P)
        for i, w in enumerate((g, u)):
            gu[:, :, :, :, i, :] = w.reshape(n, KD, P, NCH, P).transpose(0, 3, 2, 1, 4)
        o[:, :, :, 0:2 * D] = gu.reshape(n, NCH, P, 2 * D)
        o[:, :, :, 2 * D:] = d.reshape(n, NCH, P, D)
        return o.reshape(n * NCH, P, SW)

    ffn = chunks(a["ffn_w_gate"], a["ffn_w_up"], a["ffn_w_down"])
    moe = chunks(a["moe_w_gate"][0], a["moe_w_up"][0], a["moe_w_down"][0])

    w = a["nsa_w_in"][0]
    ho = head_order()
    at = np.cumsum([0, H * DH] + [G * DH] * 6)
    q, kc, vc, ks, vs, kw, vw = [w[:, at[i]:at[i + 1]] for i in range(7)]
    gg = w[:, at[7]:].reshape(D, H, 3)
    q = q.reshape(D, H, DH)[:, ho].reshape(D, H * DH)
    gg = gg[:, ho].transpose(0, 2, 1).reshape(D, 3 * H)
    w = np.concatenate([kc, ks, kw, vc, vs, vw, q, gg, np.zeros((D, NIN * CG - QKV), f)], 1)
    qkv = w.reshape(KD, P, NIN, CG).transpose(2, 1, 0, 3).reshape(NIN, P, SW)
    cmp = pack(a["nsa_cmp_w1"][0].reshape(32, P, HID), 3)
    w2 = a["nsa_cmp_w2"][0].reshape(2, 2, P, DH)
    for m in range(2):
        cmp[2, :, 2048 + m * P:2048 + m * P + DH] = w2[0, m]
        cmp[2, :, 2048 + m * P + DH:2048 + (m + 1) * P] = w2[0, m]
        cmp[2, :, 2304 + m * DH:2304 + (m + 1) * DH] = w2[1, m]
    nout = a["nsa_w_out"][0].reshape(H, DH, D)[ho].reshape(KD, P, D)
    nout = pack(nout, 3)

    par = np.zeros((P, NPAR), f)
    par[:, W_BX:W_BX + RT] = cols(a["lru_b_in"][0, RNN:])
    par[:, W_BG:W_BG + RT] = cols(a["lru_b_in"][0, :RNN])
    for k in range(CONV):
        par[:, W_CW + k * RT:W_CW + (k + 1) * RT] = cols(a["lru_conv_w"][0, k])
    for at_, name in ((W_CB, "lru_conv_b"), (W_BA, "lru_b_a"), (W_BI, "lru_b_i"), (W_LAM, "lru_lambda")):
        par[:, at_:at_ + RT] = cols(a[name][0])
    par[:, W_PE:W_PE + 32] = a["nsa_cmp_pe"][0].reshape(2, 16, P).transpose(2, 0, 1).reshape(P, 32)
    par[:, W_RT:W_RT + KD * E] = a["moe_w_router"][0].reshape(KD, P, E).transpose(1, 0, 2).reshape(P, KD * E)
    rows = np.stack([a["norm_mix"][0], a["lru_b_out"][0], a["norm_ffn"][0], a["norm_mix"][1], a["norm_ffn"][1],
                     a["norm_final"]])
    return {"x": a["x"], "consts": constants(), "params": par, "rows": rows, "w_lru": lru, "w_bd": bd,
            "w_lout": lout, "w_ffn": ffn, "w_qkv": qkv, "w_cmp": cmp, "w_nout": nout, "w_moe": moe}


def kernel(**inputs):
    import numpy as np
    import concourse.bacc as bacc
    from concourse.bass_utils import run_bass_kernel_spmd as run

    nc = bacc.Bacc("TRN2", target_bir_lowering=False, num_devices=1, dynamic_dma_scratch_size=256)
    arrays, args = {}, []
    for name, v in lay_out({k: np.asarray(v) for k, v in inputs.items()}).items():
        v = np.ascontiguousarray(v)
        arrays[f"in_{name}"] = v
        args.append(nc.dram_tensor(f"in_{name}", v.shape, mybir.dt.from_np(v.dtype), kind="ExternalInput").ap())
    args.append(nc.dram_tensor("out_0", (1, S, D), F32, kind="ExternalOutput").ap())
    build(nc, *args)
    r = run(nc, [arrays], core_ids=[0])
    return r.results[0]["out_0"]
```
